# Optimizing a Trainium2 kernel written in Bass

```python
import math
import jax, jax.numpy as jnp
from jax import lax
import numpy as np

D_MODEL = 2048
BATCH = 1
SEQ = 256
DEPTH = 1

CHUNK = 64
EPS = 1e-6
M_HEADS = 8
M_HEAD_DIM = D_MODEL // M_HEADS
M_WIDTH = M_HEADS * M_HEAD_DIM
M_CONV = 4
A_HEADS = 8
A_QK_DIM = D_MODEL // (2 * A_HEADS * 2) * 2
A_V_DIM = 2 * A_QK_DIM
A_QK_WIDTH = A_HEADS * 2 * A_QK_DIM
A_WIDTH = A_HEADS * A_V_DIM
Q_BLOCK = 128
ALIBI_SLOPES = 2.0 ** (-8.0 * np.arange(1, A_HEADS + 1) / A_HEADS)
D_FF = 5632
FF_CONV = 3
IN_SIZES = (2 * M_WIDTH,
            M_WIDTH,
            M_WIDTH,
            2 * M_HEADS,
            A_QK_WIDTH,
            A_QK_WIDTH,
            A_WIDTH,
            2 * D_MODEL)
IN_TOTAL = int(sum(IN_SIZES))
IN_SPLITS = [int(s) for s in np.cumsum(IN_SIZES)[:-1]]

kernel_name = 'hybrid_mlstm_diffattn_convffn'

def rmsnorm(x, g):
    xf = x.astype(jnp.float32)
    y = xf * lax.rsqrt(jnp.mean(xf * xf, axis=-1, keepdims=True) + EPS)
    return (y * g.astype(jnp.float32)).astype(x.dtype)

def head_rmsnorm(x, g):
    H, Dh = x.shape[2], x.shape[3]
    return rmsnorm(x, g.reshape(H, Dh))

def causal_dwconv(x, w, b):
    K, C = w.shape
    y = lax.conv_general_dilated(x, w[:, None, :].astype(x.dtype), window_strides=(1,),
                                 padding=[(K - 1, 0)], dimension_numbers=('NWC', 'WIO', 'NWC'),
                                 feature_group_count=C)
    return y + b.astype(x.dtype)

def mlstm_chunkwise(q, k, v, i_pre, logf):
    B, S, H, Dk = q.shape
    Dv = v.shape[-1]
    N = S // CHUNK
    f32 = jnp.float32

    def to_chunks(t):
        t = t.astype(f32).reshape((B, N, CHUNK, H) + t.shape[3:])
        return jnp.moveaxis(t, (1, 3), (0, 2))

    tri = jnp.tril(jnp.ones((CHUNK, CHUNK), bool))

    def step(carry, inp):
        C, n, m = carry
        qc, kc, vc, ic, fc = inp
        b = jnp.cumsum(fc, axis=-1)
        a = b + m[..., None]
        dmat = b[..., :, None] - b[..., None, :] + ic[..., None, :]
        dmat = jnp.where(tri, dmat, -jnp.inf)
        m_t = jnp.maximum(a, jnp.max(dmat, axis=-1))
        w_ts = jnp.exp(dmat - m_t[..., None])
        w_inter = jnp.exp(a - m_t)
        s_qk = jnp.einsum('bhtd,bhsd->bhts', qc, kc) * w_ts
        num = (jnp.einsum('bhts,bhsv->bhtv', s_qk, vc)
               + w_inter[..., None] * jnp.einsum('bhtk,bhkv->bhtv', qc, C))
        den = jnp.sum(s_qk, axis=-1) + w_inter * jnp.einsum('bhtk,bhk->bht', qc, n)
        h = num / jnp.maximum(jnp.abs(den), jnp.exp(-m_t))[..., None]
        b_last = b[..., -1]
        logw_s = b_last[..., None] - b + ic
        m_new = jnp.maximum(b_last + m, jnp.max(logw_s, axis=-1))
        ws = jnp.exp(logw_s - m_new[..., None])
        decay = jnp.exp(b_last + m - m_new)
        kw = kc * ws[..., None]
        C_new = decay[..., None, None] * C + jnp.einsum('bhsk,bhsv->bhkv', kw, vc)
        n_new = decay[..., None] * n + jnp.sum(kw, axis=2)
        return (C_new, n_new, m_new), h

    init = (jnp.zeros((B, H, Dk, Dv), f32), jnp.zeros((B, H, Dk), f32), jnp.zeros((B, H), f32))
    xs = (to_chunks(q) * (Dk ** -0.5), to_chunks(k), to_chunks(v), to_chunks(i_pre), to_chunks(logf))
    _, h = lax.scan(step, init, xs)
    return jnp.moveaxis(h, (0, 2), (1, 3)).reshape(B, S, H, Dv)

def diff_attention(q, k, v, lam):
    B, S, H, _, Dk = q.shape
    scale = Dk ** -0.5
    slopes = jnp.asarray(ALIBI_SLOPES, jnp.float32)
    lam = lam.astype(jnp.float32)
    outs = []
    for j in range(S // Q_BLOCK):
        start, end = j * Q_BLOCK, (j + 1) * Q_BLOCK
        qpos = jnp.arange(start, end)
        kpos = jnp.arange(end)
        s = jnp.einsum('bqhcd,bshcd->bhcqs', q[:, start:end], k[:, :end]).astype(jnp.float32) * scale
        dist = jnp.abs(qpos[:, None] - kpos[None, :]).astype(jnp.float32)
        allowed = (kpos[None, :] // CHUNK) <= (qpos[:, None] // CHUNK)
        s = jnp.where(allowed, s - slopes[:, None, None, None] * dist, -1e30)
        p = jax.nn.softmax(s, axis=-1)
        attn = p[:, :, 0] - lam * p[:, :, 1]
        outs.append(jnp.einsum('bhqs,bshd->bqhd', attn.astype(v.dtype), v[:, :end]))
    return jnp.concatenate(outs, axis=1)

def setup_inputs(seed: int = 0) -> dict:
    key = jax.random.key(seed)
    ks = jax.random.split(key, 24)
    f32 = jnp.float32

    def nrm(k, shape, scale):
        return jax.random.normal(k, shape, f32) * scale

    def gain(k, n):
        return 1.0 + nrm(k, (DEPTH, n), 0.02)

    b_i = nrm(ks[3], (DEPTH, M_HEADS), 0.1)
    b_f = jnp.linspace(3.0, 6.0, M_HEADS, dtype=f32)[None, :] + nrm(ks[4], (DEPTH, M_HEADS), 0.1)
    return {
        'x': nrm(ks[0], (BATCH, SEQ, D_MODEL), 1.0),
        'g_pre_mix': gain(ks[1], D_MODEL),
        'w_in': nrm(ks[2], (DEPTH, D_MODEL, IN_TOTAL), D_MODEL ** -0.5),
        'b_gates': jnp.concatenate([b_i, b_f], axis=-1),
        'm_conv_w': nrm(ks[5], (DEPTH, M_CONV, 2 * M_WIDTH), M_CONV ** -0.5),
        'm_conv_b': nrm(ks[6], (DEPTH, 2 * M_WIDTH), 0.02),
        'm_head_norm': gain(ks[7], M_WIDTH),
        'lambda_q1': nrm(ks[8], (DEPTH, A_QK_DIM), 0.1),
        'lambda_k1': nrm(ks[9], (DEPTH, A_QK_DIM), 0.1),
        'lambda_q2': nrm(ks[10], (DEPTH, A_QK_DIM), 0.1),
        'lambda_k2': nrm(ks[11], (DEPTH, A_QK_DIM), 0.1),
        'a_head_norm': gain(ks[12], A_WIDTH),
        'w_branch_m': nrm(ks[13], (DEPTH, M_WIDTH, D_MODEL), M_WIDTH ** -0.5),
        'w_branch_a': nrm(ks[14], (DEPTH, A_WIDTH, D_MODEL), A_WIDTH ** -0.5),
        'w_out': nrm(ks[15], (DEPTH, D_MODEL, D_MODEL), D_MODEL ** -0.5),
        'g_post_mix': gain(ks[16], D_MODEL),
        'g_pre_ffn': gain(ks[17], D_MODEL),
        'w_up': nrm(ks[18], (DEPTH, D_MODEL, 2 * D_FF), D_MODEL ** -0.5),
        'ffn_conv_w': nrm(ks[19], (DEPTH, FF_CONV, 2 * D_FF), FF_CONV ** -0.5),
        'ffn_conv_b': nrm(ks[20], (DEPTH, 2 * D_FF), 0.02),
        'w_down': nrm(ks[21], (DEPTH, D_FF, D_MODEL), D_FF ** -0.5),
        'g_post_ffn': gain(ks[22], D_MODEL),
    }

def reference(x, g_pre_mix, w_in, b_gates, m_conv_w, m_conv_b, m_head_norm,
              lambda_q1, lambda_k1, lambda_q2, lambda_k2, a_head_norm,
              w_branch_m, w_branch_a, w_out, g_post_mix, g_pre_ffn,
              w_up, ffn_conv_w, ffn_conv_b, w_down, g_post_ffn):
    B, S, _ = x.shape
    for l in range(DEPTH):
        lam_init = 0.8 - 0.6 * math.exp(-0.3 * l)
        h = rmsnorm(x, g_pre_mix[l])
        proj = h @ w_in[l]
        m_qk, m_v, m_o, m_if, a_q, a_k, a_v, merge = jnp.split(proj, IN_SPLITS, axis=-1)
        m_qk = jax.nn.silu(causal_dwconv(m_qk, m_conv_w[l], m_conv_b[l]))
        m_q, m_k = jnp.split(m_qk, 2, axis=-1)
        m_if = m_if.astype(jnp.float32) + b_gates[l].astype(jnp.float32)
        i_pre, f_pre = jnp.split(m_if, 2, axis=-1)
        hm = mlstm_chunkwise(m_q.reshape(B, S, M_HEADS, M_HEAD_DIM),
                             m_k.reshape(B, S, M_HEADS, M_HEAD_DIM),
                             m_v.reshape(B, S, M_HEADS, M_HEAD_DIM),
                             i_pre, jax.nn.log_sigmoid(f_pre))
        hm = head_rmsnorm(hm, m_head_norm[l]).reshape(B, S, M_WIDTH).astype(x.dtype)
        y_m = (jax.nn.sigmoid(m_o) * hm) @ w_branch_m[l]
        lam = (jnp.exp(jnp.dot(lambda_q1[l].astype(jnp.float32), lambda_k1[l].astype(jnp.float32)))
               - jnp.exp(jnp.dot(lambda_q2[l].astype(jnp.float32), lambda_k2[l].astype(jnp.float32)))
               + lam_init)
        ha = diff_attention(a_q.reshape(B, S, A_HEADS, 2, A_QK_DIM),
                            a_k.reshape(B, S, A_HEADS, 2, A_QK_DIM),
                            a_v.reshape(B, S, A_HEADS, A_V_DIM), lam)
        ha = head_rmsnorm(ha, a_head_norm[l]) * (1.0 - lam_init)
        y_a = ha.reshape(B, S, A_WIDTH) @ w_branch_a[l]
        g_m, g_a = jnp.split(jax.nn.sigmoid(merge), 2, axis=-1)
        mix = (g_m * y_m + g_a * y_a) @ w_out[l]
        x = x + rmsnorm(mix, g_post_mix[l])
        h = rmsnorm(x, g_pre_ffn[l])
        u = causal_dwconv(h @ w_up[l], ffn_conv_w[l], ffn_conv_b[l])
        gate, val = jnp.split(u, 2, axis=-1)
        y = (jax.nn.gelu(gate, approximate=True) * val) @ w_down[l]
        x = x + rmsnorm(y, g_post_ffn[l])
    return x


_drawn_inputs = setup_inputs


def setup_inputs(seed=0):
    import zlib

    import numpy as np

    out = dict(_drawn_inputs(seed))
    spreads = {}
    factors = {'m_conv_b': 8.0,
     'm_head_norm': 6.09,
     'a_head_norm': 4.23,
     'g_post_mix': 3.504,
     'g_pre_ffn': 3.415,
     'ffn_conv_b': 3.428,
     'g_post_ffn': 4.887}
    for name, (base, spread) in spreads.items():
        noise = np.random.default_rng([zlib.crc32(name.encode()), seed]).standard_normal(out[name].shape)
        drawn = base * np.exp(spread * noise) if base else spread * noise
        out[name] = __import__('jax').numpy.asarray(drawn.astype(out[name].dtype))
    for name, factor in factors.items():
        out[name] = (out[name] * factor).astype(out[name].dtype)
    return out
```

```python
from contextlib import ExitStack

import numpy as np

import concourse.bass as bass
from concourse import mybir

F32 = mybir.dt.float32
F32R = mybir.dt.float32r
ALU = mybir.AluOpType
ACT = mybir.ActivationFunctionType
AX_X = mybir.AxisListType.X
ds = bass.ds

P = 128
T = 256
TB = T // P
D = 2048
KT = D // P
HEADS = 8
HD = D // HEADS
QKD = 128
DFF = 5632
FT = DFF // P
CHUNK = 64
EPS = 1e-6
LAM_INIT = 0.2
SCALE_A = float(QKD) ** -0.5

M_Q, M_K, M_V, M_O = 0, D, 2 * D, 3 * D
M_IF = 4 * D
A_Q = M_IF + 2 * HEADS
A_K, A_V, G_M, G_A = A_Q + D, A_Q + 2 * D, A_Q + 3 * D, A_Q + 4 * D

RING = 4
UNIT = 1024
LOOKAHEAD = 3
UNITS_CHUNK = KT // 2
TURNS_MIX, U_MIX = 4, 8 * UNITS_CHUNK
TURNS_BR, U_BR = 4, 3 * UNITS_CHUNK
TURNS_OUT, U_OUT = KT // 4, 8
TURNS_UP, U_UP = DFF // 512, 2 * UNITS_CHUNK
TURNS_DOWN, U_DOWN = FT // 4, 8
BASE_MIX = 0
BASE_BR = BASE_MIX + TURNS_MIX * U_MIX
BASE_OUT = BASE_BR + TURNS_BR * U_BR
BASE_UP = BASE_OUT + TURNS_OUT * U_OUT
BASE_DOWN = BASE_UP + TURNS_UP * U_UP
UNITS = BASE_DOWN + TURNS_DOWN * U_DOWN

C_MCW, C_MCB = 0, 128
C_GPM, C_GMH, C_GAH, C_GPF = 160, 176, 192, 208
C_GB = 224
C_FCW, C_FCB = 225, 489
C_ALL = 577
CHAN_BLOCKS = ((128, 0, 0), (97, 0, 128), (88, 0, 225), (88, 0, 313), (88, 1, 0), (88, 1, 88))
F_ROW = 32
X_MS, X_RS, S_MS, S_RS = 0, 4, 6, 10
HALF = D // 2
S_ID, S_ALIBI, S_TRI, S_SLOPE, S_ALL = 0, 128, 512, 640, 648


def shape_constants():
    c = np.zeros((P, S_ALL), np.float32)
    c[:, S_ID:S_ID + P] = np.eye(P)
    q = P + np.arange(P)[:, None]
    k = np.arange(T)[None, :]
    late = np.where(k // CHUNK <= q // CHUNK, -np.abs(q - k), -1e30)
    c[:, S_ALIBI:S_ALIBI + P] = late[:, P:]
    c[:, S_ALIBI + P:S_ALIBI + P + T] = late
    s, t = np.arange(P)[:, None], np.arange(P)[None, :]
    c[:, S_TRI:S_TRI + P] = np.where(s <= t, 0.0, -1e30)
    c[:, S_SLOPE:S_SLOPE + HEADS] = 2.0 ** (-8.0 * np.arange(1, HEADS + 1) / HEADS) / SCALE_A
    return c


def channel_rows(a):
    gate_bias = np.zeros((1, P), np.float32)
    gate_bias[0, 0:HEADS] = a["b_gates"][0, 0:HEADS]
    gate_bias[0, F_ROW:F_ROW + HEADS] = a["b_gates"][0, HEADS:]
    rows = [a[n].reshape(-1, P) for n in ("m_conv_w", "m_conv_b", "g_pre_mix", "m_head_norm", "a_head_norm", "g_pre_ffn")]
    return np.concatenate(rows + [gate_bias] + [a[n].reshape(-1, P) for n in ("ffn_conv_w", "ffn_conv_b")])


def build_layer(nc, x, w_in, w_branch_m, w_branch_a, w_out, g_post_mix, w_up, w_down, g_post_ffn,
                chan_rows, lambdas, consts, out):
    w_in_v, w_bm_v, w_ba_v, w_out_v, w_up_v, w_down_v = (
        w[0].rearrange("(k p) n -> p k n", p=P) for w in (w_in, w_branch_m, w_branch_a, w_out, w_up, w_down))
    x_v = x[0].rearrange("(b p) d -> p b d", p=P)
    out_v = out[0].rearrange("(b p) d -> p b d", p=P)
    rows_dram = nc.dram_tensor("rows_dram", [3, HEADS, T], F32, kind="Internal").ap()

    ctx = ExitStack()
    with ctx:
        def sb(name, shape, dt=F32, stack=ctx):
            return stack.enter_context(nc.sbuf_tensor(name, shape, dt))

        def sem(name):
            return ctx.enter_context(nc.semaphore(name))

        raw = sb("raw", [P, RING, UNIT])
        w_hi = sb("w_hi", [P, RING, UNIT], F32R)
        w_lo = sb("w_lo", [P, RING, UNIT], F32R)
        h_hi = sb("h_hi", [P, KT, T], F32R)
        h_lo = sb("h_lo", [P, KT, T], F32R)
        chan = sb("chan", [P, C_ALL])
        shp = sb("shp", [P, S_ALL])
        stat = sb("stat", [P, 16])
        terms = sb("terms", [P, 3, 4])
        ident = shp[:, S_ID:S_ID + P]

        mix = ExitStack()
        gm = sb("gm", [P, KT, T], stack=mix)
        hm_hi = sb("hm_hi", [P, KT, T], F32R, stack=mix)
        hm_lo = sb("hm_lo", [P, KT, T], F32R, stack=mix)
        ha_hi = sb("ha_hi", [P, KT, T], F32R, stack=mix)
        ha_lo = sb("ha_lo", [P, KT, T], F32R, stack=mix)
        heads = ExitStack()
        qT = sb("qT", [P, 4, T], stack=heads)
        kT = sb("kT", [P, 4, T], stack=heads)
        v = sb("v", [P, TB, 512], stack=heads)
        og = sb("og", [P, 4, T], stack=heads)
        neg_g = sb("neg_g", [P, HEADS, T], stack=heads)
        prob = sb("prob", [P, 4, 384], stack=heads)
        attnT = sb("attnT", [P, 2, 384], stack=heads)
        on = sb("on", [P, TB, 2, HD], stack=heads)
        um = sb("um", [P, 2, TB, HEADS], stack=heads)
        ones = sb("ones", [P, 1], stack=heads)
        lam = sb("lam", [P, 4], stack=heads)
        ss = sb("ss", [P, 16], stack=heads)
        mx = sb("mx", [P, 2, 2, 2], stack=heads)
        sm = sb("sm", [P, 2, 2, 2], stack=heads)
        den2 = sb("den2", [P, 2, 2], stack=heads)
        floor2 = sb("floor2", [P, 2, 2], stack=heads)
        heads.close()
        branch = ExitStack()
        y = sb("y", [P, KT, T], stack=branch)
        ga = sb("ga", [P, 4, T], stack=branch)
        y_tmp = sb("y_tmp", [P, 4, T], stack=branch)
        ks_hi = sb("ks_hi", [P, RING, T], F32R, stack=branch)
        ks_lo = sb("ks_lo", [P, RING, T], F32R, stack=branch)
        branch.close()
        mix.close()
        x1 = sb("x1", [P, TB, D])
        act = sb("act", [P, FT, T])
        gpost = sb("gpost", [P, 1, D])
        sb("gap", [P, 5 * KT * T - TB * D - FT * T - D])
        xn = sb("xn", [P, TB, D])
        gate = xn[:, 0, :].rearrange("p (t c) -> p t c", c=T)
        poly = xn[:, 1, :].rearrange("p (t c) -> p t c", c=T)

        ps = ctx.enter_context(nc.psum_tensor("ps", [P, 8, 512], F32))

        raw_loaded = [sem(f"raw_loaded{i}") for i in range(RING)]
        raw_free = sem("raw_free")
        hi_done = sem("hi_done")
        lo_done = raw_free
        pe_done = sem("pe_done")
        x_loaded = [sem(f"x_loaded{i}") for i in range(2 * TB)]
        shp_loaded = sem("shp_loaded")
        rows_loaded = sem("rows_loaded")
        wif_loaded = sem("wif_loaded")
        lam_loaded = sem("lam_loaded")
        chanT = sem("chanT")
        chan_ready = sem("chan_ready")
        chan_raw = sem("chan_raw")
        x_ms = sem("x_ms")
        x_rs = sem("x_rs")
        xn_ready = sem("xn_ready")
        h_psum = sem("h_psum")
        h_hi_done = sem("h_hi_done")
        h_done = sem("h_done")
        wif_h = sem("wif_h")
        wif_ready = sem("wif_ready")
        gates_psum = sem("gates_psum")
        gates_sb = sem("gates_sb")
        gates_log = sem("gates_log")
        wif_zero = sem("wif_zero")
        pool_step = sem("pool_step")
        gate_io2 = sem("gate_io2")
        gates_ready = sem("gates_ready")
        lam_dots = sem("lam_dots")
        lam_exp = sem("lam_exp")
        lam_ready = sem("lam_ready")
        read_act = sem("read_act")
        read_dve = sem("read_dve")
        conv_bias = sem("conv_bias")
        conv_sum = sem("conv_sum")
        conv_tanh = sem("conv_tanh")
        qk_ready = sem("qk_ready")
        a_score = sem("a_score")
        a_max = sem("a_max")
        a_exp = sem("a_exp")
        a_prob = sem("a_prob")
        a_probT = sem("a_probT")
        a_probT_sb = sem("a_probT_sb")
        a_num = sem("a_num")
        a_ss = sem("a_ss")
        a_rs = sem("a_rs")
        a_on = sem("a_on")
        a_onT = sem("a_onT")
        a_hi = sem("a_hi")
        a_done = sem("a_done")
        m_arg = sem("m_arg")
        m_w = sem("m_w")
        m_score = sem("m_score")
        m_at = sem("m_at")
        m_num = sem("m_num")
        m_ss = sem("m_ss")
        m_d2 = sem("m_d2")
        m_rs = sem("m_rs")
        m_on = sem("m_on")
        m_onT = sem("m_onT")
        m_gated = sem("m_gated")
        m_hi = sem("m_hi")
        m_done = sem("m_done")
        ga_read = sem("ga_read")
        bm_read = sem("bm_read")
        ba_read = sem("ba_read")
        y_ready = sem("y_ready")
        ks_h = sem("ks_h")
        ks_done = sem("ks_done")
        gpost_loaded = sem("gpost_loaded")
        xres_loaded = sem("xres_loaded")
        block_done = sem("block_done")
        ms_half = sem("ms_half")
        gained = sem("gained")
        mix_rs = sem("mix_rs")
        x1_ready = sem("x1_ready")
        up_bias = sem("up_bias")
        gate_conv = sem("gate_conv")
        gate_sq = sem("gate_sq")
        gate_arg = sem("gate_arg")
        gate_tanh = sem("gate_tanh")
        gate_read = sem("gate_read")
        val_read = sem("val_read")
        act_ready = sem("act_ready")
        fin_ready = sem("fin_ready")
        stored = sem("stored")

        block = ctx.enter_context(nc.Block())

        def tile_bank(k):
            return (4, 5, 6, 2, 3, 4, 5, 6)[k // 2]

        gate_a = og[:].rearrange("p t c -> p (t c)")[0:HEADS, :]
        gate_g = neg_g[:].rearrange("p h t -> p (h t)")[0:HEADS, :]
        iT = gate_a[:, 768:1024]
        gate_log, fT = gate_g[:, 768:1024], gate_g[:, 1024:1280]
        wif_raw = v[:, 0, 0:KT * 2 * HEADS].rearrange("p (k c) -> p k c", c=2 * HEADS)
        gm_rows = gm[:].rearrange("p (b k) t -> p b (k t)", b=TB)

        def half_of(tensor, b, h):
            return tensor[:, b, h * HALF:(h + 1) * HALF]

        def ps_half(b, h):
            return ps[:, 4 * b + 2 * h:4 * b + 2 * h + 2, :].rearrange("p b c -> p (b c)")

        def units_done(n):
            return n + 1 + RING

        @block.sync
        def _(sp):
            def load(n, slot, dst_src):
                sp.wait_ge(raw_free, n + 1)
                dst, src = dst_src
                sp.dma_start(dst, src).then_inc(raw_loaded[slot], 16)

            def chunk_unit(u, view, col):
                k = 2 * (u % UNITS_CHUNK)
                return raw[:, u % RING, :].rearrange("p (k c) -> p k c", k=2), view[:, k:k + 2, ds(col, 512)]

            for b in range(TB):
                for h in range(2):
                    sp.dma_start(half_of(gm_rows, b, h), half_of(x_v, b, h)).then_inc(x_loaded[2 * b + h], 16)
            with sp.Fori(1, TURNS_MIX + 1) as turn:
                for c, base in enumerate((A_Q, A_K, A_V, M_Q, M_K, M_V, M_O, G_M)):
                    for i in range(UNITS_CHUNK):
                        u = c * UNITS_CHUNK + i
                        load(turn * U_MIX + (u - U_MIX), u % RING, chunk_unit(u, w_in_v, turn * 512 + (base - 512)))
            with sp.Fori(1, TURNS_BR + 1) as turn:
                for c, (view, base) in enumerate(((w_in_v, G_A), (w_bm_v, 0), (w_ba_v, 0))):
                    for i in range(UNITS_CHUNK):
                        u = c * UNITS_CHUNK + i
                        load(turn * U_BR + (BASE_BR - U_BR + u), u % RING, chunk_unit(u, view, turn * 512 + (base - 512)))
            with sp.Fori(1, TURNS_OUT + 1) as turn:
                for u in range(U_OUT):
                    half = u % 2 * UNIT
                    load(turn * U_OUT + (BASE_OUT - U_OUT + u), u % RING,
                         (raw[:, u % RING:u % RING + 1, :], w_out_v[:, ds(turn * 4 + (u // 2 - 4), 1), half:half + UNIT]))
            with sp.Fori(1, TURNS_UP + 1) as turn:
                for u in range(U_UP):
                    col = turn * 512 + ((DFF if u >= UNITS_CHUNK else 0) - 512)
                    load(turn * U_UP + (BASE_UP - U_UP + u), u % RING, chunk_unit(u, w_up_v, col))
            with sp.Fori(1, TURNS_DOWN + 1) as turn:
                for u in range(U_DOWN):
                    half = u % 2 * UNIT
                    load(turn * U_DOWN + (BASE_DOWN - U_DOWN + u), u % RING,
                         (raw[:, u % RING:u % RING + 1, :], w_down_v[:, ds(turn * 4 + (u // 2 - 4), 1), half:half + UNIT]))
            for b in range(TB):
                for h in range(2):
                    sp.wait_ge(fin_ready, 2 * b + h + 1)
                    sp.dma_start(half_of(out_v, b, h), half_of(xn, b, h)).then_inc(stored, 16)
            sp.wait_ge(stored, 16 * 2 * TB)

        @block.gpsimd
        def _(pool):
            steps = [0]

            def then(ins):
                steps[0] += 1
                ins.then_inc(pool_step, 1)
                pool.wait_ge(pool_step, steps[0])

            def root(out_ap, in_ap, eps):
                n = out_ap.shape[1]
                nc.gpsimd.tensor_tensor(out_ap, in_ap, terms[:, eps, 0:n], ALU.add)
                pool.drain()
                return nc.gpsimd.tensor_tensor(out_ap, out_ap, terms[:, 0, 0:n], ALU.pow)

            nc.gpsimd.memset(ones[:], 1.0)
            nc.gpsimd.memset(terms[:, 0, :], -0.5)
            nc.gpsimd.memset(terms[:, 1, :], EPS)
            then(nc.gpsimd.memset(terms[:, 2, :], 1e-37))
            for part in (hm_hi, hm_lo):
                ins = nc.gpsimd.memset(part[:, :, 0:P].bitcast(F32), 0.0)
            ins.then_inc(wif_zero, 1)

            def inverse_root(column, ready, count, out_column, done):
                pool.wait_ge(ready, count)
                nc.gpsimd.tensor_tensor(stat[:, column:column + 1], stat[:, column:column + 1],
                                        stat[:, column + 1:column + 2], ALU.add)
                pool.drain()
                root(stat[:, out_column:out_column + 1], stat[:, column:column + 1], 1).then_inc(done, 1)

            for b in range(TB):
                inverse_root(X_MS + 2 * b, x_ms, 2 * b + 2, X_RS + b, x_rs)

            PADS = 128
            a0, a1 = gate_a[:, 0:384], gate_a[:, 384:768]
            g0, g1 = gate_g[:, 0:384], gate_g[:, 384:768]
            then(nc.gpsimd.memset(gate_a[:, 0:768], 0.0))
            then(nc.gpsimd.memset(gate_g[:, 0:768], 0.0))
            pool.wait_ge(gates_log, 1)
            then(nc.gpsimd.tensor_scalar(a0[:, PADS:], fT, 0.0, None, ALU.min))
            then(nc.gpsimd.tensor_tensor(a0[:, PADS:], a0[:, PADS:], gate_log, ALU.subtract))
            src, dst = a0, a1
            for k in (1, 2, 4, 8, 16, 32, 64, 128):
                then(nc.gpsimd.tensor_tensor(dst[:, PADS:], src[:, PADS:], src[:, PADS - k:384 - k], ALU.add))
                src, dst = dst, src
            F, rise = src[:, PADS:], dst[:, PADS:]
            then(nc.gpsimd.tensor_tensor(iT, iT, F, ALU.subtract))
            then(nc.gpsimd.tensor_scalar(g0[:, PADS:], iT, 0.0, None, ALU.max))
            src, dst = g0, g1
            for k in (1, 2, 4, 8, 16, 32, 64, 128):
                then(nc.gpsimd.tensor_tensor(rise, src[:, PADS - k:384 - k], src[:, PADS:], ALU.subtract))
                then(nc.gpsimd.tensor_scalar(rise, rise, 0.0, None, ALU.max))
                then(nc.gpsimd.tensor_tensor(dst[:, PADS:], src[:, PADS:], rise, ALU.add))
                src, dst = dst, src
            then(nc.gpsimd.tensor_tensor(F, F, src[:, PADS:], ALU.add))
            then(nc.gpsimd.tensor_scalar(F, F, -40.0, None, ALU.max))
            then(nc.gpsimd.tensor_scalar(src[:, PADS:], src[:, PADS:], -1.0, None, ALU.mult))
            for row, val in enumerate((src[:, PADS:], iT, F)):
                pool.dma_start(rows_dram[row], val).then_inc(gate_io2, 16)
            pool.wait_ge(gate_io2, 48)
            pool.dma_start(neg_g[:].rearrange("p h t -> p (h t)"),
                           rows_dram[0].rearrange("h t -> (h t)").partition_broadcast(P)).then_inc(gates_ready, 16)
            with nc.allow_non_contiguous_dma("gates by token, a few thousand elements"):
                for which in range(2):
                    for b in range(TB):
                        pool.dma_start(um[:, which, b, :], rows_dram[1 + which][:, b * P:(b + 1) * P].rearrange("h p -> p h")
                                       ).then_inc(gates_ready, 16)

            with pool.Fori(0, TURNS_MIX) as g:
                pool.wait_ge(a_ss, g + 1)
                root(ss[:, 4:8], ss[:, 0:4], 1).then_inc(a_rs, 1)
                pool.wait_ge(m_d2, g + 1)
                pool.wait_ge(m_ss, g + 1)
                den = den2[:].rearrange("p j b -> p (j b)")
                nc.gpsimd.tensor_tensor(den, den, terms[:, 1, :], ALU.mult)
                pool.drain()
                nc.gpsimd.tensor_tensor(ss[:, 8:12], ss[:, 8:12], den, ALU.add)
                pool.drain()
                root(ss[:, 12:16], ss[:, 8:12], 2).then_inc(m_rs, 1)

            for b in range(TB):
                inverse_root(S_MS + 2 * b, ms_half, 2 * b + 2, S_RS + b, mix_rs)
            for b in range(TB):
                inverse_root(X_MS + 2 * b, x_ms, 2 * TB + 2 * b + 2, X_RS + b, x_rs)
            for b in range(TB):
                inverse_root(S_MS + 2 * b, ms_half, 2 * TB + 2 * b + 2, S_RS + b, mix_rs)

        @block.scalar
        def _(scalar):
            def copy(out_ap, in_ap, scale=1.0):
                return nc.scalar.activation(out_ap, in_ap, ACT.Copy, scale=scale)

            def split(n4, n, slot):
                scalar.wait_ge(raw_loaded[slot], n4 * 16 + 16)
                scalar.wait_ge(pe_done, n + 1)
                copy(w_hi[:, slot, :], raw[:, slot, :]).then_inc(hi_done, 1)

            def split_ahead(turn, per_turn, base, u):
                u += LOOKAHEAD
                split(turn * (per_turn // RING) + (base + u) // RING, turn * per_turn + (base + u), u % RING)

            def banks(lo, n, k):
                return ps[:, lo:lo + n, :].rearrange("p b (t c) -> p (b t) c", c=k)

            def norm_tiles(count, gain):
                for k in range(KT):
                    if k % 2 == 0:
                        scalar.wait_ge(h_psum, (count + k) // 2 + 1)
                    ins = copy(h_hi[:, k, :], ps[:, tile_bank(k), k % 2 * T:k % 2 * T + T],
                               scale=chan[:, gain + k:gain + k + 1])
                    if k % 2:
                        ins.then_inc(h_hi_done, 1)

            def squares_out(n, tensor=act):
                return tensor[:, 4 * n:4 * n + 4, :].rearrange("p t c -> p (t c)")

            def square_half(src, junk, column, done):
                nc.scalar.activation(junk, src, ACT.Square, scale=float(D) ** -0.5,
                                     accum_out=stat[:, column:column + 1]).then_inc(done, 1)

            nc.scalar.sem_inc(read_act, 2)
            nc.scalar.sem_inc(ga_read, 1)
            scalar.dma_start(shp[:], consts).then_inc(shp_loaded, 16)
            stage = prob[:].rearrange("p a b -> p (a b)").rearrange("p (k c) -> p k c", c=P)
            row = 0
            for k, (rows, _, _) in enumerate(CHAN_BLOCKS[0:2]):
                scalar.dma_start(stage[0:rows, k, :], chan_rows[row:row + rows, :]).then_inc(rows_loaded, 16)
                row += rows
            scalar.dma_start(stage[0:88, 2:6, :], chan_rows[row:row + 4 * 88, :].rearrange("(k r) c -> r k c", k=4)
                             ).then_inc(rows_loaded, 16)
            scalar.dma_start(wif_raw, w_in_v[:, :, M_IF:M_IF + 2 * HEADS]).then_inc(wif_loaded, 16)
            lams = on[:].rearrange("p a b c -> p (a b c)")
            scalar.dma_start(lams[:, 0:4 * QKD], lambdas.partition_broadcast(P)).then_inc(lam_loaded, 16)

            for b in range(TB):
                for h in range(2):
                    scalar.wait_ge(x_loaded[2 * b + h], 16)
                    square_half(half_of(gm_rows, b, h), squares_out(2 * b + h, ha_hi), X_MS + 2 * b + h, x_ms)
                if b == 0:
                    scalar.wait_ge(chanT, 1)
                    copy(chan[:, 0:401], ps[:, 0, 0:401])
                    copy(chan[:, 401:577], ps[:, 1, 0:176]).then_inc(chan_raw, 1)
            scalar.wait_ge(wif_loaded, 16)
            scalar.wait_ge(wif_zero, 1)
            copy(hm_hi[:, :, 0:HEADS], wif_raw[:, :, 0:HEADS])
            copy(hm_hi[:, :, F_ROW:F_ROW + HEADS], wif_raw[:, :, HEADS:]).then_inc(wif_h, 1)
            for u in range(LOOKAHEAD):
                split(0, u, u)
            scalar.wait_ge(chan_ready, 1)
            norm_tiles(0, C_GPM)
            scalar.wait_ge(gates_psum, 1)
            nc.scalar.activation(iT, ps[0:HEADS, 7, 0:T], ACT.Identity, bias=chan[0:HEADS, C_GB:C_GB + 1])
            nc.scalar.activation(fT, ps[F_ROW:F_ROW + HEADS, 7, 0:T], ACT.Identity,
                                 bias=chan[F_ROW:F_ROW + HEADS, C_GB:C_GB + 1]).then_inc(gates_sb, 1)
            scalar.drain()
            nc.scalar.activation(gate_log, fT, ACT.Abs)
            scalar.drain()
            nc.scalar.activation(gate_log, gate_log, ACT.Exp, scale=-1.0)
            scalar.drain()
            nc.scalar.activation(gate_log, gate_log, ACT.Ln, bias=1.0).then_inc(gates_log, 1)
            scalar.wait_ge(lam_dots, 1)
            nc.scalar.activation(lam[:, 0:2], lam[:, 0:2], ACT.Exp).then_inc(lam_exp, 1)

            def conv_terms(g, c, pair, dst, tiles):
                for t in tiles:
                    tile = g * 4 + (t + (KT if c == 4 else 0))
                    nc_in = ps[:, 2 * pair + t // 2, t % 2 * T:t % 2 * T + T]
                    ins = nc.scalar.activation(dst[:, t, :], nc_in, ACT.Identity, bias=chan[:, ds(tile + C_MCB, 1)],
                                               scale=chan[:, ds(tile + (C_MCW + 96), 1)])
                ins.then_inc(conv_bias, 1)

            with scalar.Fori(0, TURNS_MIX) as g:
                for u in range(U_MIX):
                    split_ahead(g, U_MIX, BASE_MIX, u)
                    if u == 7:
                        scalar.wait_ge(pe_done, g * U_MIX + units_done(u))
                        copy(qT[:], banks(0, 2, T)).then_inc(read_act, 1)
                    if u == 15:
                        scalar.wait_ge(pe_done, g * U_MIX + units_done(u))
                        copy(kT[:], banks(2, 2, T)).then_inc(read_act, 1)
                    if u == 23:
                        scalar.wait_ge(pe_done, g * U_MIX + units_done(u))
                        copy(v[:], banks(0, 2, 512)).then_inc(read_act, 1)
                    if u in (19, 20):
                        j = u - 19
                        scalar.wait_ge(a_max, g * 2 + (j + 1))
                        for m in range(2):
                            for blk, (c0, c1) in enumerate(((0, 128), (128, 384))):
                                ins = nc.scalar.activation(prob[:, 2 * j + m, c0:c1], prob[:, 2 * j + m, c0:c1], ACT.Exp,
                                                           bias=mx[:, j, blk, m:m + 1], scale=SCALE_A,
                                                           accum_out=sm[:, j, blk, m:m + 1])
                        ins.then_inc(a_exp, 1)
                    if u == 22:
                        scalar.wait_ge(a_probT, g + 1)
                        copy(attnT[:], ps[:, 4:6, 0:384]).then_inc(a_probT_sb, 1)
                    if u == 26:
                        scalar.wait_ge(a_num, g + 1)
                        for j in range(2):
                            for b in range(TB):
                                ins = nc.scalar.activation(on[:, b, j, :], ps[:, 6 + j, b * HD:b * HD + HD], ACT.Square,
                                                           scale=float(HD) ** -0.5, accum_out=ss[:, 2 * j + b:2 * j + b + 1])
                        ins.then_inc(a_ss, 1)
                    if u == 34:
                        scalar.wait_ge(a_onT, g + 1)
                        for t in range(4):
                            ins = nc.scalar.activation(ha_hi[:, ds(g * 4 + t, 1), :],
                                                       ps[:, 4 + t // 2:5 + t // 2, t % 2 * T:t % 2 * T + T], ACT.Copy,
                                                       scale=chan[:, ds(g * 4 + (C_GAH + t), 1)])
                        ins.then_inc(a_hi, 1)
                    if u in (31, 32, 39, 40):
                        c = 3 if u < 35 else 4
                        dst = qT if c == 3 else kT
                        t0 = 0 if u % 8 == 7 else 2
                        if t0 == 0:
                            scalar.wait_ge(pe_done, g * U_MIX + units_done(u))
                        conv_terms(g, c, c % 2, dst, (t0, t0 + 1))
                    if u in (33, 41):
                        dst = qT if u == 33 else kT
                        scalar.wait_ge(conv_sum, g * 4 + (2 if u == 33 else 4))
                        nc.scalar.activation(prob[:].rearrange("p a b -> p (a b)")[:, 0:4 * T],
                                             dst[:].rearrange("p t c -> p (t c)"), ACT.Tanh, scale=0.5).then_inc(conv_tanh, 1)
                    if u == 43:
                        scalar.wait_ge(m_arg, g + 1)
                        for j in range(2):
                            for b, (c0, c1) in enumerate(((0, 256), (256, 384))):
                                ins = nc.scalar.activation(prob[:, j, c0:c1], prob[:, j, c0:c1], ACT.Exp,
                                                           bias=um[:, 0, b, ds(g * 2 + j, 1)])
                        ins.then_inc(m_w, 1)
                    if u == 47:
                        scalar.wait_ge(pe_done, g * U_MIX + units_done(u))
                        copy(v[:], banks(2, 2, 512)).then_inc(read_act, 1)
                    if u == 51:
                        scalar.wait_ge(m_num, g + 1)
                        for j in range(2):
                            for b in range(TB):
                                ins = nc.scalar.activation(on[:, b, j, :], ps[:, 6 + j, b * HD:b * HD + HD], ACT.Square,
                                                           scale=float(HD) ** -0.5, accum_out=ss[:, 8 + 2 * j + b:9 + 2 * j + b])
                        nc.scalar.activation(floor2[:], um[:, 1, :, ds(g * 2, 2)].rearrange("p b j -> p j b"), ACT.Exp,
                                             scale=-2.0).then_inc(m_ss, 1)
                    if u == 55:
                        scalar.wait_ge(pe_done, g * U_MIX + units_done(u))
                        nc.scalar.activation(og[:], banks(0, 2, T), ACT.Tanh, scale=0.5).then_inc(read_act, 1)
                    if u == 59:
                        scalar.wait_ge(m_gated, g + 2)
                        tmp = prob[:].rearrange("p a b -> p (a b)")[:, 0:4 * T].rearrange("p (t c) -> p t c", c=T)
                        for t in range(4):
                            ins = nc.scalar.activation(hm_hi[:, ds(g * 4 + t, 1), :], tmp[:, t:t + 1, :], ACT.Copy,
                                                       scale=chan[:, ds(g * 4 + (C_GMH + t), 1)])
                        ins.then_inc(m_hi, 1)
                    if u == 63:
                        scalar.wait_ge(pe_done, g * U_MIX + units_done(u))
                        nc.scalar.activation(gm[:, ds(g * 4, 4), :], banks(2, 2, T), ACT.Tanh, scale=0.5).then_inc(read_act, 1)

            with scalar.Fori(0, TURNS_BR) as g:
                for u in range(U_BR):
                    split_ahead(g, U_BR, BASE_BR, u)
                    if u == 7:
                        scalar.wait_ge(pe_done, g * U_BR + units_done(BASE_BR + u))
                        scalar.wait_ge(y_ready, g + 1)
                        nc.scalar.activation(ga[:], banks(4, 2, T), ACT.Tanh, scale=0.5).then_inc(ga_read, 1)

            def rows_phase(turns, per_turn, base, src, scale, src_ready, then_load):
                for k in range(2):
                    copy(ks_hi[:, k:k + 1, :], src[:, k:k + 1, :], scale=scale).then_inc(ks_h, 1)

                def turn(g, first, last):
                    for u in range(per_turn):
                        if not (last and u + LOOKAHEAD >= per_turn):
                            split_ahead(g, per_turn, base, u)
                        k = u // 2 + 2
                        if u == 4:
                            scalar.wait_ge(*src_ready)
                            if first:
                                then_load()
                        if u % 2 == 0 and not (last and k >= 4):
                            copy(ks_hi[:, k % RING:k % RING + 1, :], src[:, ds(g * 4 + k, 1), :], scale=scale).then_inc(ks_h, 1)

                turn(0, True, False)
                with scalar.Fori(1, turns - 1) as g:
                    turn(g, False, False)
                turn(turns - 1, False, True)

            def load_residual():
                scalar.dma_start(x1[:], x_v).then_inc(xres_loaded, 16)
                scalar.dma_start(gpost[:, 0, :], g_post_mix[0].partition_broadcast(P)).then_inc(gpost_loaded, 16)

            scalar.wait_ge(y_ready, 2)
            rows_phase(TURNS_OUT, U_OUT, BASE_OUT, y, 0.5, (y_ready, TURNS_BR + 1), load_residual)

            def output_squares(b, count, last_unit):
                if b == 0:
                    scalar.wait_ge(block_done, count // TB + 1)
                else:
                    scalar.wait_ge(pe_done, units_done(last_unit))
                for h in range(2):
                    if h:
                        scalar.wait_ge(gained, 2 * (count + b) + 1)
                    square_half(ps_half(b, h), squares_out(2 * b + h), S_MS + 2 * b + h, ms_half)

            output_squares(0, 0, None)
            for u in range(LOOKAHEAD):
                split(BASE_UP // RING, BASE_UP + u, u)
            output_squares(1, 0, BASE_UP - 1)
            for b in range(TB):
                for h in range(2):
                    scalar.wait_ge(x1_ready, 2 * b + h + 1)
                    square_half(half_of(x1, b, h), squares_out(4 + 2 * b + h), X_MS + 2 * b + h, x_ms)
            norm_tiles(KT, C_GPF)

            def up_terms(g, first_tile, pair, dst):
                for t in range(4):
                    tile = g * 4 + (first_tile + t)
                    ins = nc.scalar.activation(dst[:, t, :], ps[:, 2 * pair + t // 2, t % 2 * T:t % 2 * T + T], ACT.Identity,
                                               bias=chan[:, ds(tile + C_FCB, 1)], scale=chan[:, ds(tile + (C_FCW + 176), 1)])
                    if t % 2:
                        ins.then_inc(up_bias, 1)

            with scalar.Fori(0, TURNS_UP) as g:
                for u in range(U_UP):
                    split_ahead(g, U_UP, BASE_UP, u)
                    if u == 7:
                        scalar.wait_ge(pe_done, g * U_UP + units_done(BASE_UP + u))
                        scalar.wait_ge(act_ready, g + 1)
                        up_terms(g, 0, 0, gate)
                    if u == 9:
                        scalar.wait_ge(gate_read, g * 2 + 3)
                        nc.scalar.activation(poly[:, 0:4, :], gate[:, 0:4, :], ACT.Square).then_inc(gate_sq, 1)
                    if u == 11:
                        scalar.wait_ge(gate_arg, g + 1)
                        nc.scalar.activation(poly[:, 0:4, :], poly[:, 0:4, :], ACT.Tanh,
                                             scale=(2.0 / np.pi) ** 0.5).then_inc(gate_tanh, 1)
                    if u == 15:
                        scalar.wait_ge(pe_done, g * U_UP + units_done(BASE_UP + u))
                        up_terms(g, FT, 1, gate[:, 4:8, :])

            def load_gain():
                scalar.dma_start(gpost[:, 0, :], g_post_ffn[0].partition_broadcast(P)).then_inc(gpost_loaded, 16)

            rows_phase(TURNS_DOWN, U_DOWN, BASE_DOWN, act, 1.0, (act_ready, TURNS_UP + 1), load_gain)
            for b in range(TB):
                output_squares(b, TB, UNITS - 1)

        @block.vector
        def _(vec):
            def stt(out_ap, in0, scalar, in1, op0, op1):
                return nc.vector.scalar_tensor_tensor(out=out_ap, in0=in0, scalar=scalar, in1=in1, op0=op0, op1=op1)

            def split(n, slot):
                vec.wait_ge(hi_done, n + 1)
                nc.vector.tensor_tensor(w_lo[:, slot, :], raw[:, slot, :], w_hi[:, slot, :].bitcast(F32),
                                        ALU.subtract).then_inc(lo_done, 1)

            def split_ahead(turn, per_turn, base, u):
                u += LOOKAHEAD
                split(turn * per_turn + (base + u), u % RING)

            def norm_tiles(count, gain, after_half=None):
                for k in range(KT):
                    if k == KT // 2 and after_half:
                        after_half()
                    if k % 2 == 0:
                        vec.wait_ge(h_hi_done, (count + k) // 2 + 1)
                    stt(h_lo[:, k, :], ps[:, tile_bank(k), k % 2 * T:k % 2 * T + T], chan[:, gain + k:gain + k + 1],
                        h_hi[:, k, :].bitcast(F32), ALU.mult, ALU.subtract).then_inc(h_done, 1)

            nc.vector.sem_inc(raw_free, RING)
            for starts_at_one in (m_gated, y_ready, bm_read, ba_read, gate_read, val_read, act_ready):
                nc.vector.sem_inc(starts_at_one, 1)
            vec.wait_ge(chan_raw, 1)
            nc.vector.tensor_scalar(chan[:, C_GMH:C_GMH + KT], chan[:, C_GMH:C_GMH + KT], 0.5, None, ALU.mult)
            nc.vector.tensor_scalar(chan[:, C_GAH:C_GAH + KT], chan[:, C_GAH:C_GAH + KT], 1.0 - LAM_INIT, None,
                                    ALU.mult).then_inc(chan_ready, 1)
            for b in range(TB):
                vec.wait_ge(x_rs, b + 1)
                nc.vector.tensor_scalar(gm_rows[:, b, :], gm_rows[:, b, :], stat[:, X_RS + b:X_RS + b + 1], None,
                                        ALU.mult).then_inc(xn_ready, 1)
            vec.wait_ge(wif_h, 1)
            for col, c0 in ((0, 0), (F_ROW, HEADS)):
                ins = nc.vector.tensor_tensor(hm_lo[:, :, col:col + HEADS], wif_raw[:, :, c0:c0 + HEADS],
                                              hm_hi[:, :, col:col + HEADS].bitcast(F32), ALU.subtract)
            ins.then_inc(wif_ready, 1)
            for u in range(LOOKAHEAD):
                split(u, u)
            norm_tiles(0, C_GPM)
            vec.wait_ge(lam_loaded, 16)
            lams = on[:].rearrange("p a b c -> p (a b c)")
            nc.vector.tensor_tensor(lams[:, 512:768], lams[:, 0:256], lams[:, 256:512], ALU.mult)
            vec.drain()
            nc.vector.reduce_sum(lam[:, 0:2], lams[:, 512:768].rearrange("p (a c) -> p a c", a=2), AX_X).then_inc(lam_dots, 1)
            vec.wait_ge(lam_exp, 1)
            stt(lam[:, 2:3], lam[:, 1:2], -LAM_INIT, lam[:, 0:1], ALU.add, ALU.subtract)
            vec.drain()

            alibi = shp[:, S_ALIBI:S_ALIBI + 384].unsqueeze(1).broadcast_to([P, 2, 384])
            tri = shp[:, S_TRI:S_TRI + P].unsqueeze(1).broadcast_to([P, 2, P])
            flat = prob[:].rearrange("p a b -> p (a b)")

            def conv_taps(g, c, pair, dst, tiles, taps, first_tile, weight, stride):
                for j in range(1, taps):
                    for t in tiles:
                        tile = g * 4 + (first_tile + t)
                        off = t % 2 * T
                        ins = stt(dst[:, t, j:], ps[:, 2 * pair + t // 2, off:off + T - j],
                                  chan[:, ds(tile + (weight + (taps - 1 - j) * stride), 1)], dst[:, t, j:], ALU.mult, ALU.add)
                    if j < taps - 1:
                        vec.drain()
                return ins

            with vec.Fori(0, TURNS_MIX) as g:
                for u in range(U_MIX):
                    split_ahead(g, U_MIX, BASE_MIX, u)
                    if u in (18, 19):
                        j = u - 18
                        vec.wait_ge(a_score, g * 2 + (j + 1))
                        stt(prob[:, 2 * j:2 * j + 2, :], alibi, shp[:, ds(g * 2 + (S_SLOPE + j), 1)],
                            ps[:, 4 + 2 * j:6 + 2 * j, 0:384], ALU.mult, ALU.add)
                        vec.drain()
                        nc.vector.reduce_max(mx[:, j, 0, :], prob[:, 2 * j:2 * j + 2, 0:128], AX_X)
                        nc.vector.reduce_max(mx[:, j, 1, :], prob[:, 2 * j:2 * j + 2, 128:384], AX_X)
                        vec.drain()
                        nc.vector.tensor_scalar(mx[:, j, :, :], mx[:, j, :, :], -SCALE_A, None, ALU.mult).then_inc(a_max, 1)
                    if u in (20, 21):
                        j = u - 20
                        vec.wait_ge(a_exp, g * 2 + (j + 1))
                        nc.vector.reciprocal(sm[:, j, :, :], sm[:, j, :, :])
                        vec.drain()
                        nc.vector.tensor_scalar(sm[:, j, :, 1:2], sm[:, j, :, 1:2], lam[:, 2:3], None, ALU.mult)
                        for blk, (c0, c1) in enumerate(((0, 128), (128, 384))):
                            nc.vector.tensor_scalar(prob[:, 2 * j, c0:c1], prob[:, 2 * j, c0:c1], sm[:, j, blk, 0:1], None, ALU.mult)
                        vec.drain()
                        for blk, (c0, c1) in enumerate(((0, 128), (128, 384))):
                            ins = stt(prob[:, 2 * j, c0:c1], prob[:, 2 * j + 1, c0:c1], sm[:, j, blk, 1:2],
                                      prob[:, 2 * j, c0:c1], ALU.mult, ALU.add)
                        ins.then_inc(a_prob, 1)
                    if u == 26:
                        vec.wait_ge(a_rs, g + 1)
                        for j in range(2):
                            for b in range(TB):
                                ins = nc.vector.tensor_scalar(on[:, b, j, :], ps[:, 6 + j, b * HD:b * HD + HD],
                                                              ss[:, 4 + 2 * j + b:5 + 2 * j + b], None, ALU.mult)
                        ins.then_inc(a_on, 1)
                    if u == 35:
                        vec.wait_ge(a_hi, g + 1)
                        for t in range(4):
                            ins = stt(ha_lo[:, ds(g * 4 + t, 1), :], ps[:, 4 + t // 2:5 + t // 2, t % 2 * T:t % 2 * T + T],
                                      chan[:, ds(g * 4 + (C_GAH + t), 1)], ha_hi[:, ds(g * 4 + t, 1), :].bitcast(F32),
                                      ALU.mult, ALU.subtract)
                        ins.then_inc(a_done, 1)
                    if u in (31, 32, 39, 40):
                        c = 3 if u < 35 else 4
                        t0 = 0 if u % 8 == 7 else 2
                        vec.wait_ge(conv_bias, g * 4 + ((c - 3) * 2 + t0 // 2 + 1))
                        ins = conv_taps(g, c, c % 2, qT if c == 3 else kT, (t0, t0 + 1), 4, (c - 3) * KT, C_MCW, 32)
                        ins.then_inc(conv_sum, 1)
                        if t0 == 2:
                            vec.drain().then_inc(read_dve, 1)
                    if u in (34, 42):
                        dst = (qT if u == 34 else kT)[:].rearrange("p t c -> p (t c)")
                        vec.wait_ge(conv_tanh, g * 2 + (1 if u == 34 else 2))
                        stt(dst, flat[:, 0:4 * T], 1.0, dst, ALU.add, ALU.mult).then_inc(qk_ready, 1)
                    if u == 42:
                        vec.drain()
                        vec.wait_ge(gates_ready, 80)
                        for j in range(2):
                            row = neg_g[:, ds(g * 2 + j, 1), :]
                            w3 = prob[:, j, :].rearrange("p (b c) -> p b c", c=P)
                            nc.vector.tensor_tensor(w3[:, 0:3:2, :], row.rearrange("p a (b c) -> p (a b) c", c=P), tri, ALU.add)
                            ins = nc.vector.tensor_copy(prob[:, j:j + 1, P:2 * P], row[:, :, P:2 * P])
                        ins.then_inc(m_arg, 1)
                    if u == 46:
                        vec.wait_ge(m_w, g + 1)
                        vec.wait_ge(m_score, g + 1)
                        for j in range(2):
                            ins = stt(prob[:, 2 + j, :], ps[:, 4 + j, 0:384], 0.25 * float(HD) ** -0.5, prob[:, j, :],
                                      ALU.mult, ALU.mult)
                        ins.then_inc(m_at, 1)
                    if u == 51:
                        vec.wait_ge(m_num, g + 1)
                        nc.vector.tensor_copy(den2[:], ps[:, 4:6, 384:386])
                        vec.drain()
                        nc.vector.tensor_tensor(den2[:], den2[:], den2[:], ALU.mult)
                        vec.drain()
                        vec.wait_ge(m_ss, g + 1)
                        nc.vector.tensor_tensor(den2[:], den2[:], floor2[:], ALU.max).then_inc(m_d2, 1)
                    if u == 53:
                        vec.wait_ge(m_rs, g + 1)
                        for j in range(2):
                            for b in range(TB):
                                ins = nc.vector.tensor_scalar(on[:, b, j, :], ps[:, 6 + j, b * HD:b * HD + HD],
                                                              ss[:, 12 + 2 * j + b:13 + 2 * j + b], None, ALU.mult)
                        ins.then_inc(m_on, 1)
                    if u == 59:
                        vec.wait_ge(m_onT, g + 1)
                        vec.wait_ge(read_act, g * 6 + 7)
                        stt(flat[:, 0:4 * T].rearrange("p (a b) -> p a b", a=2), og[:].rearrange("p (a t) c -> p a (t c)", a=2),
                            1.0, ps[:, 4:6, :], ALU.add, ALU.mult).then_inc(m_gated, 1)
                    if u == 60:
                        vec.wait_ge(m_hi, g + 1)
                        tmp = flat[:, 0:4 * T].rearrange("p (t c) -> p t c", c=T)
                        for t in range(4):
                            ins = stt(hm_lo[:, ds(g * 4 + t, 1), :], tmp[:, t:t + 1, :], chan[:, ds(g * 4 + (C_GMH + t), 1)],
                                      hm_hi[:, ds(g * 4 + t, 1), :].bitcast(F32), ALU.mult, ALU.subtract)
                        ins.then_inc(m_done, 1)

            def halves(ap):
                return ap.rearrange("p (a t) c -> p a (t c)", a=2)

            def branch_sum(g):
                vec.wait_ge(pe_done, g * U_BR + units_done(BASE_BR + U_BR - 1))
                vec.wait_ge(ga_read, g + 2)
                stt(halves(y_tmp[:]), halves(ga[:]), 1.0, ps[:, 2:4, :], ALU.add, ALU.mult).then_inc(ba_read, 1)
                vec.drain()
                nc.vector.tensor_tensor(y[:, ds(g * 4, 4), :], y[:, ds(g * 4, 4), :], y_tmp[:], ALU.add).then_inc(y_ready, 1)

            def branch_turn(g, last):
                for u in range(U_BR):
                    split_ahead(g, U_BR, BASE_BR, u)
                    if u == 15:
                        vec.wait_ge(pe_done, g * U_BR + units_done(BASE_BR + u))
                        vec.wait_ge(read_act, 6 * TURNS_MIX + 2)
                        stt(halves(y[:, ds(g * 4, 4), :]), halves(gm[:, ds(g * 4, 4), :]), 1.0, ps[:, 0:2, :],
                            ALU.add, ALU.mult).then_inc(bm_read, 1)
                    if u == 23 and not last:
                        branch_sum(g)

            with vec.Fori(0, TURNS_BR - 1) as g:
                branch_turn(g, False)
            branch_turn(TURNS_BR - 1, True)

            def rows_phase(turns, per_turn, base, src, scale, tiles_before, rest):
                def lo(k, slot, count):
                    vec.wait_ge(ks_h, count)
                    stt(ks_lo[:, slot:slot + 1, :], src[:, k, :], scale, ks_hi[:, slot:slot + 1, :].bitcast(F32),
                        ALU.mult, ALU.subtract).then_inc(ks_done, 1)

                for k in range(2):
                    lo(slice(k, k + 1), k, tiles_before + k + 1)
                rest()

                def turn(g, last):
                    for u in range(per_turn):
                        if not (last and u + LOOKAHEAD >= per_turn):
                            split_ahead(g, per_turn, base, u)
                        k = u // 2 + 2
                        if u % 2 == 0 and not (last and k >= 4):
                            lo(ds(g * 4 + k, 1), k % RING, g * 4 + (tiles_before + k + 1))

                with vec.Fori(0, turns - 1) as g:
                    turn(g, False)
                turn(turns - 1, True)

            rows_phase(TURNS_OUT, U_OUT, BASE_OUT, y, 0.5, 0, lambda: branch_sum(TURNS_BR - 1))
            def gain_halves(b, count, last_unit):
                if b == 0:
                    vec.wait_ge(block_done, count // TB + 1)
                else:
                    vec.wait_ge(pe_done, units_done(last_unit))
                for h in (1, 0):
                    if h == 0:
                        vec.wait_ge(ms_half, 2 * (count + b) + 1)
                    nc.vector.tensor_tensor(half_of(xn, b, h), ps_half(b, h), half_of(gpost, 0, h), ALU.mult).then_inc(gained, 1)
                vec.drain()

            def residual(b, count, dst, done):
                vec.wait_ge(mix_rs, count + b + 1)
                for h in range(2):
                    stt(half_of(dst, b, h), half_of(xn, b, h), stat[:, S_RS + b:S_RS + b + 1], half_of(x1, b, h),
                        ALU.mult, ALU.add).then_inc(done, 1)

            vec.wait_ge(gpost_loaded, 16)
            vec.wait_ge(xres_loaded, 16)
            gain_halves(0, 0, None)
            residual(0, 0, x1, x1_ready)
            split(BASE_UP, 0)
            gain_halves(1, 0, BASE_UP - 1)
            residual(1, 0, x1, x1_ready)
            for b in range(TB):
                vec.wait_ge(x_rs, TB + b + 1)
                nc.vector.tensor_scalar(xn[:, b, :], x1[:, b, :], stat[:, X_RS + b:X_RS + b + 1], None,
                                        ALU.mult).then_inc(xn_ready, 1)
                if b == 0:
                    split(BASE_UP + 1, 1)
            norm_tiles(KT, C_GPF, lambda: split(BASE_UP + 2, 2))

            def value_tail(g):
                vec.wait_ge(up_bias, g * 4 + 4)
                conv_taps(g, 1, 1, gate[:, 4:8, :], (2, 3), 3, FT, C_FCW, 88).then_inc(val_read, 1)
                vec.drain()
                stt(act[:, ds(g * 4, 4), :], gate[:, 0:4, :], 0.5, gate[:, 4:8, :], ALU.mult, ALU.mult).then_inc(act_ready, 1)

            def up_turn(g, first):
                for u in range(U_UP):
                    split_ahead(g, U_UP, BASE_UP, u)
                    if u == 0 and not first:
                        value_tail(g - 1)
                    if u in (7, 8):
                        vec.wait_ge(up_bias, g * 4 + (u - 6))
                        conv_taps(g, 0, 0, gate, ((0, 1), (2, 3))[u - 7], 3, 0, C_FCW, 88).then_inc(gate_read, 1)
                    if u == 10:
                        vec.wait_ge(gate_sq, g + 1)
                        nc.vector.tensor_scalar(poly[:, 0:4, :], poly[:, 0:4, :], 0.044715, 1.0, ALU.mult, ALU.add)
                        vec.drain()
                        nc.vector.tensor_tensor(poly[:, 0:4, :], poly[:, 0:4, :], gate[:, 0:4, :], ALU.mult).then_inc(gate_arg, 1)
                    if u == 12:
                        vec.wait_ge(gate_tanh, g + 1)
                        stt(gate[:, 0:4, :], poly[:, 0:4, :], 1.0, gate[:, 0:4, :], ALU.add, ALU.mult)
                    if u == 15:
                        vec.wait_ge(up_bias, g * 4 + 3)
                        conv_taps(g, 1, 1, gate[:, 4:8, :], (0, 1), 3, FT, C_FCW, 88)

            up_turn(0, True)
            with vec.Fori(1, TURNS_UP) as g:
                up_turn(g, False)
            rows_phase(TURNS_DOWN, U_DOWN, BASE_DOWN, act, 1.0, KT, lambda: value_tail(TURNS_UP - 1))
            vec.wait_ge(gpost_loaded, 32)
            for b in range(TB):
                gain_halves(b, TB, UNITS - 1)
                residual(b, TB, xn, fin_ready)

        @block.tensor
        def _(pe):
            def three(out_ap, stat_hi, stat_lo, mov_hi, mov_lo, start, stop):
                nc.tensor.matmul(out_ap, stat_hi, mov_hi, start=start, stop=False, skip_group_check=True)
                nc.tensor.matmul(out_ap, stat_hi, mov_lo, start=False, stop=False, skip_group_check=True)
                return nc.tensor.matmul(out_ap, stat_lo, mov_hi, start=False, stop=stop, skip_group_check=True)

            def ready(n):
                pe.wait_ge(lo_done, n + 1 + RING)

            def unit_channels(u, pair, a_hi_t, a_lo_t):
                slot = u % RING
                for kk in range(2):
                    k = 2 * (u % UNITS_CHUNK) + kk
                    for t in range(4):
                        c = kk * 512 + t * P
                        last = three(ps[:, 2 * pair + t // 2, t % 2 * T:t % 2 * T + T],
                                     w_hi[:, slot, c:c + P], w_lo[:, slot, c:c + P], a_hi_t[:, k, :], a_lo_t[:, k, :],
                                     start=k == 0 and t % 2 == 0, stop=k == KT - 1)
                last.then_inc(pe_done, 1)

            def unit_tokens(u, pair):
                slot = u % RING
                for kk in range(2):
                    k = 2 * (u % UNITS_CHUNK) + kk
                    for b in range(TB):
                        last = three(ps[:, 2 * pair + b, :], h_hi[:, k, b * P:(b + 1) * P], h_lo[:, k, b * P:(b + 1) * P],
                                     w_hi[:, slot, kk * 512:kk * 512 + 512], w_lo[:, slot, kk * 512:kk * 512 + 512],
                                     start=k == 0, stop=k == KT - 1)
                last.then_inc(pe_done, 1)

            def transposes(src, count):
                pe.wait_ge(xn_ready, count // KT * TB + TB)
                for k in range(KT):
                    if k % 2 == 0 and k >= 10:
                        pe.wait_ge(h_done, count + k - 10 + 2)
                    for b in range(TB):
                        last = nc.tensor.transpose(ps[:, tile_bank(k), k % 2 * T + b * P:k % 2 * T + (b + 1) * P],
                                                   src[:, b, k * P:(k + 1) * P], ident)
                    if k % 2:
                        last.then_inc(h_psum, 1)

            def head_values(weights, j):
                for b, parts in ((0, ((0, 0),)), (1, ((1, 0), (2, 1)))):
                    for i, (part, s) in enumerate(parts):
                        last = nc.tensor.matmul(ps[:, 6 + j, b * HD:(b + 1) * HD], weights[:, part * P:(part + 1) * P],
                                                v[:, s, j * HD:(j + 1) * HD], start=i == 0, stop=i == len(parts) - 1)
                return last

            def heads_out():
                for t in range(4):
                    for b in range(TB):
                        last = nc.tensor.transpose(ps[:, 4 + t // 2, t % 2 * T + b * P:t % 2 * T + (b + 1) * P],
                                                   on[:, b, t // 2, t % 2 * P:(t % 2 + 1) * P], ident)
                return last

            nc.tensor.sem_inc(pe_done, RING)
            stage = prob[:].rearrange("p a b -> p (a b)").rearrange("p (k c) -> p k c", c=P)
            pe.wait_ge(shp_loaded, 16)
            pe.wait_ge(rows_loaded, 16 * 3)
            for k, (rows, bank, col) in enumerate(CHAN_BLOCKS):
                last = nc.tensor.transpose(ps[:, bank, col:col + rows], stage[0:rows, k, :], ident[0:rows, 0:rows])
            last.then_inc(chanT, 1)
            transposes(gm_rows, 0)
            pe.wait_ge(wif_ready, 1)
            for k in range(KT):
                pe.wait_ge(h_done, k + 1)
                last = three(ps[:, 7, 0:T], hm_hi[:, k, 0:P], hm_lo[:, k, 0:P], h_hi[:, k, :], h_lo[:, k, :],
                             start=k == 0, stop=k == KT - 1)
            last.then_inc(gates_psum, 1)

            with pe.Fori(0, TURNS_MIX) as g:
                for u in range(U_MIX):
                    c = u // UNITS_CHUNK
                    if u % UNITS_CHUNK == 0:
                        if c in (5, 6):
                            pe.wait_ge(read_dve, g * 2 + (c - 4))
                        else:
                            pe.wait_ge(read_act, g * 6 + (c + 1 if c < 5 else 6))
                    ready(g * U_MIX + (BASE_MIX + u))
                    if c in (2, 5):
                        unit_tokens(u, c % 2)
                    else:
                        unit_channels(u, c % 2, h_hi, h_lo)
                    if u == 17:
                        pe.wait_ge(read_act, g * 6 + 4)
                        pe.wait_ge(m_gated, g + 1)
                        pe.wait_ge(gates_sb, 1)
                        for j in range(2):
                            for m in range(2):
                                q, k = qT[:, 2 * j + m, :], kT[:, 2 * j + m, :]
                                bank = 4 + 2 * j + m
                                nc.tensor.matmul(ps[:, bank, 0:P], q[:, 0:P], k[:, 0:P], start=True, stop=True)
                                last = nc.tensor.matmul(ps[:, bank, P:P + T], q[:, P:T], k[:, 0:T], start=True, stop=True)
                            last.then_inc(a_score, 1)
                    if u == 22:
                        pe.wait_ge(a_prob, g * 2 + 2)
                        for j in range(2):
                            for b in range(3):
                                last = nc.tensor.transpose(ps[:, 4 + j, b * P:(b + 1) * P], prob[:, 2 * j, b * P:(b + 1) * P], ident)
                        last.then_inc(a_probT, 1)
                    if u == 25:
                        pe.wait_ge(a_probT_sb, g + 1)
                        pe.wait_ge(read_act, g * 6 + 5)
                        for j in range(2):
                            last = head_values(attnT[:, j, :], j)
                        last.then_inc(a_num, 1)
                    if u == 32:
                        pe.wait_ge(a_on, g + 1)
                        heads_out().then_inc(a_onT, 1)
                    if u == 45:
                        pe.wait_ge(qk_ready, g * 2 + 2)
                        pe.wait_ge(a_done, g + 1)
                        for j in range(2):
                            for s in range(2):
                                for dt in range(2):
                                    last = nc.tensor.matmul(ps[:, 4 + j, (0, 256)[s]:(256, 384)[s]],
                                                            kT[:, 2 * j + dt, s * P:(s + 1) * P], qT[:, 2 * j + dt, s * P:T],
                                                            start=dt == 0, stop=dt == 1)
                        last.then_inc(m_score, 1)
                    if u == 50:
                        pe.wait_ge(m_at, g + 1)
                        pe.wait_ge(read_act, g * 6 + 6)
                        for j in range(2):
                            head_values(prob[:, 2 + j, :], j)
                            for b, parts in ((0, (0,)), (1, (1, 2))):
                                for i, part in enumerate(parts):
                                    last = nc.tensor.matmul(ps[:, 4 + j, 384 + b:385 + b], prob[:, 2 + j, part * P:(part + 1) * P],
                                                            ones[:], start=i == 0, stop=i == len(parts) - 1)
                        last.then_inc(m_num, 1)
                    if u == 57:
                        pe.wait_ge(m_on, g + 1)
                        heads_out().then_inc(m_onT, 1)

            with pe.Fori(0, TURNS_BR) as g:
                for u in range(U_BR):
                    c = u // UNITS_CHUNK
                    if u == 0:
                        pe.wait_ge(ga_read, g + 1)
                        pe.wait_ge(m_gated, TURNS_MIX + 1)
                    if u == 8:
                        pe.wait_ge(bm_read, g + 1)
                        pe.wait_ge(read_act, 6 * TURNS_MIX + 1)
                        pe.wait_ge(m_done, TURNS_MIX)
                    if u == 16:
                        pe.wait_ge(ba_read, g + 1)
                        pe.wait_ge(read_act, 6 * TURNS_MIX + 2)
                        pe.wait_ge(a_done, TURNS_MIX)
                    ready(g * U_BR + (BASE_BR + u))
                    unit_channels(u, (2, 0, 1)[c], *((h_hi, h_lo), (hm_hi, hm_lo), (ha_hi, ha_lo))[c])

            def rows_unit(u, b, first, last):
                slot, kslot = u % RING, u // 2 % RING
                for part in (ks_hi, ks_lo):
                    for n in range(2):
                        a = part[:, kslot, b * P:(b + 1) * P]
                        o = ps[:, 4 * b + u % 2 * 2 + n, :]
                        ins = nc.tensor.matmul(o, a, w_hi[:, slot, n * 512:n * 512 + 512], start=first and part is ks_hi,
                                               stop=last and part is ks_lo, skip_group_check=True)
                        if part is ks_hi:
                            nc.tensor.matmul(o, a, w_lo[:, slot, n * 512:n * 512 + 512],
                                             start=False, stop=False, skip_group_check=True)
                return ins

            def rows_phase(turns, per_turn, base, tiles_before, bank_waits):
                def waits(g, u, first):
                    if first and u < 2:
                        bank_waits(u)
                    if u % 2 == 0:
                        pe.wait_ge(ks_done, g * 4 + (tiles_before + u // 2 + 1))
                    ready(g * per_turn + (base + u))

                def turn(g, first, units):
                    for u in units:
                        waits(g, u, first)
                        for b in range(TB):
                            ins = rows_unit(u, b, first and u < 2, False)
                        ins.then_inc(pe_done, 1)

                turn(0, True, range(per_turn))
                with pe.Fori(1, turns - 1) as g:
                    turn(g, False, range(per_turn))
                turn(turns - 1, False, range(RING))
                for u in range(RING, 2 * RING):
                    waits(turns - 1, u, False)
                    ins = rows_unit(u, 0, False, u >= per_turn - 2)
                ins.then_inc(block_done, 1)
                for u in range(RING, 2 * RING):
                    rows_unit(u, 1, False, u >= per_turn - 2).then_inc(pe_done, 1)

            def out_banks(u):
                if u == 0:
                    pe.wait_ge(ga_read, TURNS_BR + 1)
                    pe.wait_ge(bm_read, TURNS_BR + 1)
                    pe.wait_ge(m_on, TURNS_MIX)
                else:
                    pe.wait_ge(ba_read, TURNS_BR + 1)

            rows_phase(TURNS_OUT, U_OUT, BASE_OUT, 0, out_banks)
            transposes(xn, KT)
            with pe.Fori(0, TURNS_UP) as g:
                for u in range(U_UP):
                    if u == 0:
                        pe.wait_ge(gate_read, g * 2 + 1)
                    if u == 8:
                        pe.wait_ge(val_read, g + 1)
                    if u < UNITS_CHUNK:
                        pe.wait_ge(h_done, KT + 2 * u + 2)
                    ready(g * U_UP + (BASE_UP + u))
                    unit_channels(u, u // UNITS_CHUNK, h_hi, h_lo)

            def down_banks(u):
                pe.wait_ge(*((gate_read, 2 * TURNS_UP + 1) if u == 0 else (val_read, TURNS_UP + 1)))

            rows_phase(TURNS_DOWN, U_DOWN, BASE_DOWN, KT, down_banks)


_INS = ['x', 'w_in', 'w_branch_m', 'w_branch_a', 'w_out', 'g_post_mix', 'w_up', 'w_down', 'g_post_ffn']


def kernel(**inputs):
    import concourse.bacc as bacc
    from concourse.bass_utils import run_bass_kernel_spmd

    nc = bacc.Bacc("TRN2", target_bir_lowering=False, num_devices=1)
    arrays, args = {}, []
    inputs = {name: np.ascontiguousarray(a) for name, a in inputs.items()}
    laid = {name: inputs[name] for name in _INS}
    laid["channel_rows"] = channel_rows(inputs)
    laid["lambdas"] = np.concatenate([inputs[n][0] for n in ("lambda_q1", "lambda_q2", "lambda_k1", "lambda_k2")])
    laid["shape_constants"] = shape_constants()
    for name, a in laid.items():
        arrays[f"in_{name}"] = a
        args.append(nc.dram_tensor(f"in_{name}", a.shape, mybir.dt.from_np(a.dtype), kind="ExternalInput").ap())
    args.append(nc.dram_tensor("out", (1, T, D), F32, kind="ExternalOutput").ap())
    build_layer(nc, *args)
    r = run_bass_kernel_spmd(nc, [arrays], core_ids=[0])
    return r.results[0]["out"]
```

```python
from contextlib import ExitStack

import numpy as np

import concourse.bass as bass
from concourse import mybir

F32 = mybir.dt.float32
F32R = mybir.dt.float32r
ALU = mybir.AluOpType
ACT = mybir.ActivationFunctionType
AX_X = mybir.AxisListType.X
ds = bass.ds

P = 128
T = 256
TB = T // P
D = 2048
KT = D // P
HEADS = 8
HD = D // HEADS
QKD = 128
DFF = 5632
FT = DFF // P
CHUNK = 64
EPS = 1e-6
LAM_INIT = 0.2
SCALE_A = float(QKD) ** -0.5

M_Q, M_K, M_V, M_O = 0, D, 2 * D, 3 * D
M_IF = 4 * D
A_Q = M_IF + 2 * HEADS
A_K, A_V, G_M, G_A = A_Q + D, A_Q + 2 * D, A_Q + 3 * D, A_Q + 4 * D

RING = 4
UNIT = 1024
LOOKAHEAD = 3
UNITS_CHUNK = KT // 2
TURNS_MIX, U_MIX = 4, 8 * UNITS_CHUNK
TURNS_BR, U_BR = 4, 3 * UNITS_CHUNK
TURNS_OUT, U_OUT = KT // 4, 8
TURNS_UP, U_UP = DFF // 512, 2 * UNITS_CHUNK
TURNS_DOWN, U_DOWN = FT // 4, 8
BASE_MIX = 0
BASE_BR = BASE_MIX + TURNS_MIX * U_MIX
BASE_OUT = BASE_BR + TURNS_BR * U_BR
BASE_UP = BASE_OUT + TURNS_OUT * U_OUT
BASE_DOWN = BASE_UP + TURNS_UP * U_UP
UNITS = BASE_DOWN + TURNS_DOWN * U_DOWN

C_MCW, C_MCB = 0, 128
C_GPM, C_GMH, C_GAH, C_GPF = 160, 176, 192, 208
C_GB = 224
C_FCW, C_FCB = 225, 489
C_ALL = 577
CHAN_BLOCKS = ((128, 0, 0), (97, 0, 128), (88, 0, 225), (88, 0, 313), (88, 1, 0), (88, 1, 88))
F_ROW = 32
X_MS, X_RS, S_MS, S_RS = 0, 4, 6, 10
HALF = D // 2
S_ID, S_ALIBI, S_TRI, S_SLOPE, S_ALL = 0, 128, 512, 640, 648


def shape_constants():
    c = np.zeros((P, S_ALL), np.float32)
    c[:, S_ID:S_ID + P] = np.eye(P)
    q = P + np.arange(P)[:, None]
    k = np.arange(T)[None, :]
    late = np.where(k // CHUNK <= q // CHUNK, -np.abs(q - k), -1e30)
    c[:, S_ALIBI:S_ALIBI + P] = late[:, P:]
    c[:, S_ALIBI + P:S_ALIBI + P + T] = late
    s, t = np.arange(P)[:, None], np.arange(P)[None, :]
    c[:, S_TRI:S_TRI + P] = np.where(s <= t, 0.0, -1e30)
    c[:, S_SLOPE:S_SLOPE + HEADS] = 2.0 ** (-8.0 * np.arange(1, HEADS + 1) / HEADS) / SCALE_A
    return c


def channel_rows(a):
    gate_bias = np.zeros((1, P), np.float32)
    gate_bias[0, 0:HEADS] = a["b_gates"][0, 0:HEADS]
    gate_bias[0, F_ROW:F_ROW + HEADS] = a["b_gates"][0, HEADS:]
    rows = [a[n].reshape(-1, P) for n in ("m_conv_w", "m_conv_b", "g_pre_mix", "m_head_norm", "a_head_norm", "g_pre_ffn")]
    return np.concatenate(rows + [gate_bias] + [a[n].reshape(-1, P) for n in ("ffn_conv_w", "ffn_conv_b")])


def build_layer(nc, x, w_in, w_branch_m, w_branch_a, w_out, g_post_mix, w_up, w_down, g_post_ffn,
                chan_rows, lambdas, consts, out):
    w_in_v, w_bm_v, w_ba_v, w_out_v, w_up_v, w_down_v = (
        w[0].rearrange("(k p) n -> p k n", p=P) for w in (w_in, w_branch_m, w_branch_a, w_out, w_up, w_down))
    x_v = x[0].rearrange("(b p) d -> p b d", p=P)
    out_v = out[0].rearrange("(b p) d -> p b d", p=P)
    rows_dram = nc.dram_tensor("rows_dram", [3, HEADS, T], F32, kind="Internal").ap()

    ctx = ExitStack()
    with ctx:
        def sb(name, shape, dt=F32, stack=ctx):
            return stack.enter_context(nc.sbuf_tensor(name, shape, dt))

        def sem(name):
            return ctx.enter_context(nc.semaphore(name))

        raw = sb("raw", [P, RING, UNIT])
        w_hi = sb("w_hi", [P, RING, UNIT], F32R)
        w_lo = sb("w_lo", [P, RING, UNIT], F32R)
        h_hi = sb("h_hi", [P, KT, T], F32R)
        h_lo = sb("h_lo", [P, KT, T], F32R)
        chan = sb("chan", [P, C_ALL])
        shp = sb("shp", [P, S_ALL])
        stat = sb("stat", [P, 16])
        terms = sb("terms", [P, 3, 4])
        ident = shp[:, S_ID:S_ID + P]

        mix = ExitStack()
        gm = sb("gm", [P, KT, T], stack=mix)
        hm_hi = sb("hm_hi", [P, KT, T], F32R, stack=mix)
        hm_lo = sb("hm_lo", [P, KT, T], F32R, stack=mix)
        ha_hi = sb("ha_hi", [P, KT, T], F32R, stack=mix)
        ha_lo = sb("ha_lo", [P, KT, T], F32R, stack=mix)
        heads = ExitStack()
        qT = sb("qT", [P, 4, T], stack=heads)
        kT = sb("kT", [P, 4, T], stack=heads)
        v = sb("v", [P, TB, 512], stack=heads)
        og = sb("og", [P, 4, T], stack=heads)
        neg_g = sb("neg_g", [P, HEADS, T], stack=heads)
        prob = sb("prob", [P, 4, 384], stack=heads)
        attnT = sb("attnT", [P, 2, 384], stack=heads)
        on = sb("on", [P, TB, 2, HD], stack=heads)
        um = sb("um", [P, 2, TB, HEADS], stack=heads)
        ones = sb("ones", [P, 1], stack=heads)
        lam = sb("lam", [P, 4], stack=heads)
        ss = sb("ss", [P, 16], stack=heads)
        mx = sb("mx", [P, 2, 2, 2], stack=heads)
        sm = sb("sm", [P, 2, 2, 2], stack=heads)
        den2 = sb("den2", [P, 2, 2], stack=heads)
        floor2 = sb("floor2", [P, 2, 2], stack=heads)
        heads.close()
        branch = ExitStack()
        y = sb("y", [P, KT, T], stack=branch)
        ga = sb("ga", [P, 4, T], stack=branch)
        y_tmp = sb("y_tmp", [P, 4, T], stack=branch)
        ks_hi = sb("ks_hi", [P, RING, T], F32R, stack=branch)
        ks_lo = sb("ks_lo", [P, RING, T], F32R, stack=branch)
        branch.close()
        mix.close()
        x1 = sb("x1", [P, TB, D])
        act = sb("act", [P, FT, T])
        gpost = sb("gpost", [P, 1, D])
        sb("gap", [P, 5 * KT * T - TB * D - FT * T - D])
        xn = sb("xn", [P, TB, D])
        gate = xn[:, 0, :].rearrange("p (t c) -> p t c", c=T)
        poly = xn[:, 1, :].rearrange("p (t c) -> p t c", c=T)

        ps = ctx.enter_context(nc.psum_tensor("ps", [P, 8, 512], F32))

        raw_loaded = [sem(f"raw_loaded{i}") for i in range(RING)]
        raw_free = sem("raw_free")
        hi_done = sem("hi_done")
        lo_done = raw_free
        pe_done = sem("pe_done")
        x_loaded = [sem(f"x_loaded{i}") for i in range(2 * TB)]
        shp_loaded = sem("shp_loaded")
        rows_loaded = sem("rows_loaded")
        wif_loaded = sem("wif_loaded")
        lam_loaded = sem("lam_loaded")
        chanT = sem("chanT")
        chan_ready = sem("chan_ready")
        chan_raw = sem("chan_raw")
        x_ms = sem("x_ms")
        x_rs = sem("x_rs")
        xn_ready = sem("xn_ready")
        h_psum = sem("h_psum")
        h_hi_done = sem("h_hi_done")
        h_done = sem("h_done")
        wif_h = sem("wif_h")
        wif_ready = sem("wif_ready")
        gates_psum = sem("gates_psum")
        gates_sb = sem("gates_sb")
        gates_log = sem("gates_log")
        wif_zero = sem("wif_zero")
        pool_step = sem("pool_step")
        gate_io2 = sem("gate_io2")
        gates_ready = sem("gates_ready")
        lam_dots = sem("lam_dots")
        lam_exp = sem("lam_exp")
        lam_ready = sem("lam_ready")
        read_act = sem("read_act")
        read_dve = sem("read_dve")
        conv_bias = sem("conv_bias")
        conv_sum = sem("conv_sum")
        conv_tanh = sem("conv_tanh")
        qk_ready = sem("qk_ready")
        a_score = sem("a_score")
        a_max = sem("a_max")
        a_exp = sem("a_exp")
        a_prob = sem("a_prob")
        a_probT = sem("a_probT")
        a_probT_sb = sem("a_probT_sb")
        a_num = sem("a_num")
        a_ss = sem("a_ss")
        a_rs = sem("a_rs")
        a_on = sem("a_on")
        a_onT = sem("a_onT")
        a_hi = sem("a_hi")
        a_done = sem("a_done")
        m_arg = sem("m_arg")
        m_w = sem("m_w")
        m_score = sem("m_score")
        m_at = sem("m_at")
        m_num = sem("m_num")
        m_ss = sem("m_ss")
        m_d2 = sem("m_d2")
        m_rs = sem("m_rs")
        m_on = sem("m_on")
        m_onT = sem("m_onT")
        m_gated = sem("m_gated")
        m_hi = sem("m_hi")
        m_done = sem("m_done")
        ga_read = sem("ga_read")
        bm_read = sem("bm_read")
        ba_read = sem("ba_read")
        y_ready = sem("y_ready")
        ks_h = sem("ks_h")
        ks_done = sem("ks_done")
        gpost_loaded = sem("gpost_loaded")
        xres_loaded = sem("xres_loaded")
        half_done = sem("half_done")
        ms_half = sem("ms_half")
        gained = sem("gained")
        mix_rs = sem("mix_rs")
        x1_ready = sem("x1_ready")
        up_bias = sem("up_bias")
        gate_conv = sem("gate_conv")
        gate_sq = sem("gate_sq")
        gate_arg = sem("gate_arg")
        gate_tanh = sem("gate_tanh")
        gate_read = sem("gate_read")
        val_read = sem("val_read")
        act_ready = sem("act_ready")
        fin_ready = sem("fin_ready")
        stored = sem("stored")

        block = ctx.enter_context(nc.Block())

        def tile_bank(k):
            return (2, 3, 4, 5, 6, 2, 3, 4)[k // 2]

        gate_a = og[:].rearrange("p t c -> p (t c)")[0:HEADS, :]
        gate_g = neg_g[:].rearrange("p h t -> p (h t)")[0:HEADS, :]
        iT = gate_a[:, 768:1024]
        gate_log, fT = gate_g[:, 768:1024], gate_g[:, 1024:1280]
        wif_raw = v[:, 0, 0:KT * 2 * HEADS].rearrange("p (k c) -> p k c", c=2 * HEADS)
        chan_stage = prob[:].rearrange("p a b -> p (a b)").rearrange("p (k c) -> p k c", c=P)
        gm_rows = gm[:].rearrange("p (b k) t -> p b (k t)", b=TB)

        h_units = [part[:].rearrange("p k t -> p (k t)").rearrange("p (s c) -> p s c", c=UNIT) for part in (h_hi, h_lo)]

        def half_of(tensor, b, h):
            return tensor[:, b, h * HALF:(h + 1) * HALF]

        def ps_half(b, h):
            return ps[:, 4 * b + 2 * h:4 * b + 2 * h + 2, :].rearrange("p b c -> p (b c)")

        def rows_place(u, by_halves):
            return (u % 4, u // 4) if by_halves else (u // 2, u % 2)

        def last_split(u):
            hi, lo = (w_hi, w_lo) if u < RING else (h_units[0], h_units[1])
            return hi[:, u % RING, :], lo[:, u % RING, :]

        def next_tile(u, first, last):
            if first:
                return {5: 4, 6: 5, 7: 6}.get(u)
            if last:
                return {0: 3}.get(u)
            return u // 2 + 3 if u % 2 == 0 else None

        def units_done(n):
            return n + 1 + RING

        @block.sync
        def _(sp):
            def load(n, slot, dst_src):
                sp.wait_ge(raw_free, n + 1)
                dst, src = dst_src
                sp.dma_start(dst, src).then_inc(raw_loaded[slot], 16)

            def chunk_unit(u, view, col):
                k = 2 * (u % UNITS_CHUNK)
                return raw[:, u % RING, :].rearrange("p (k c) -> p k c", k=2), view[:, k:k + 2, ds(col, 512)]

            def rows_loads(turns, per_turn, base, view):
                for u in range(per_turn):
                    k, half = rows_place(u, True)
                    load(base + u, u % RING, (raw[:, u % RING:u % RING + 1, :],
                                              view[:, k:k + 1, half * UNIT:(half + 1) * UNIT]))
                with sp.Fori(1, turns - 1) as turn:
                    for u in range(per_turn):
                        k, half = rows_place(u, False)
                        load(turn * per_turn + (base + u), u % RING,
                             (raw[:, u % RING:u % RING + 1, :],
                              view[:, ds(turn * 4 + k, 1), half * UNIT:(half + 1) * UNIT]))
                for u in range(per_turn):
                    k, half = rows_place(u, True)
                    k += (turns - 1) * 4
                    load((turns - 1) * per_turn + base + u, u % RING,
                         (raw[:, u % RING:u % RING + 1, :], view[:, k:k + 1, half * UNIT:(half + 1) * UNIT]))

            for b in range(TB):
                for h in range(2):
                    sp.dma_start(half_of(gm_rows, b, h), half_of(x_v, b, h)).then_inc(x_loaded[2 * b + h], 16)
            row = 0
            for k, (rows, _, _) in enumerate(CHAN_BLOCKS[0:2]):
                sp.dma_start(chan_stage[0:rows, k, :], chan_rows[row:row + rows, :]).then_inc(rows_loaded, 16)
                row += rows
            sp.dma_start(chan_stage[0:88, 2:6, :], chan_rows[row:row + 4 * 88, :].rearrange("(k r) c -> r k c", k=4)
                         ).then_inc(rows_loaded, 16)
            sp.dma_start(wif_raw, w_in_v[:, :, M_IF:M_IF + 2 * HEADS]).then_inc(wif_loaded, 16)
            with sp.Fori(1, TURNS_MIX + 1) as turn:
                for c, base in enumerate((A_Q, A_K, A_V, M_Q, M_K, M_V, M_O, G_M)):
                    for i in range(UNITS_CHUNK):
                        u = c * UNITS_CHUNK + i
                        load(turn * U_MIX + (u - U_MIX), u % RING, chunk_unit(u, w_in_v, turn * 512 + (base - 512)))
            with sp.Fori(1, TURNS_BR + 1) as turn:
                for c, (view, base) in enumerate(((w_in_v, G_A), (w_bm_v, 0), (w_ba_v, 0))):
                    for i in range(UNITS_CHUNK):
                        u = c * UNITS_CHUNK + i
                        load(turn * U_BR + (BASE_BR - U_BR + u), u % RING, chunk_unit(u, view, turn * 512 + (base - 512)))
            rows_loads(TURNS_OUT, U_OUT, BASE_OUT, w_out_v)
            with sp.Fori(1, TURNS_UP + 1) as turn:
                for u in range(U_UP):
                    col = turn * 512 + ((DFF if u >= UNITS_CHUNK else 0) - 512)
                    load(turn * U_UP + (BASE_UP - U_UP + u), u % RING, chunk_unit(u, w_up_v, col))
            rows_loads(TURNS_DOWN, U_DOWN, BASE_DOWN, w_down_v)
            for b in range(TB):
                for h in range(2):
                    sp.wait_ge(fin_ready, 2 * b + h + 1)
                    sp.dma_start(half_of(out_v, b, h), half_of(xn, b, h)).then_inc(stored, 16)
            sp.wait_ge(stored, 16 * 2 * TB)

        @block.gpsimd
        def _(pool):
            steps = [0]

            def then(ins):
                steps[0] += 1
                ins.then_inc(pool_step, 1)
                pool.wait_ge(pool_step, steps[0])

            def root(out_ap, in_ap, eps):
                n = out_ap.shape[1]
                nc.gpsimd.tensor_tensor(out_ap, in_ap, terms[:, eps, 0:n], ALU.add)
                pool.drain()
                return nc.gpsimd.tensor_tensor(out_ap, out_ap, terms[:, 0, 0:n], ALU.pow)

            nc.gpsimd.memset(ones[:], 1.0)
            nc.gpsimd.memset(terms[:, 0, :], -0.5)
            nc.gpsimd.memset(terms[:, 1, :], EPS)
            then(nc.gpsimd.memset(terms[:, 2, :], 1e-37))
            for part in (hm_hi, hm_lo):
                ins = nc.gpsimd.memset(part[:, :, 0:P].bitcast(F32), 0.0)
            ins.then_inc(wif_zero, 1)

            def inverse_root(column, ready, count, out_column, done):
                pool.wait_ge(ready, count)
                nc.gpsimd.tensor_scalar(stat[:, column:column + 1], stat[:, column:column + 1],
                                        stat[:, column + 1:column + 2], EPS, ALU.add, ALU.add)
                pool.drain()
                nc.gpsimd.tensor_tensor(stat[:, out_column:out_column + 1], stat[:, column:column + 1],
                                        terms[:, 0, 0:1], ALU.pow).then_inc(done, 1)

            for b in range(TB):
                inverse_root(X_MS + 2 * b, x_ms, 2 * b + 2, X_RS + b, x_rs)

            PADS = 128
            a0, a1 = gate_a[:, 0:384], gate_a[:, 384:768]
            g0, g1 = gate_g[:, 0:384], gate_g[:, 384:768]
            then(nc.gpsimd.memset(gate_a[:, 0:768], 0.0))
            then(nc.gpsimd.memset(gate_g[:, 0:768], 0.0))
            pool.wait_ge(gates_log, 1)
            then(nc.gpsimd.tensor_scalar(a0[:, PADS:], fT, 0.0, None, ALU.min))
            then(nc.gpsimd.tensor_tensor(a0[:, PADS:], a0[:, PADS:], gate_log, ALU.subtract))
            src, dst = a0, a1
            for k in (1, 2, 4, 8, 16, 32, 64, 128):
                then(nc.gpsimd.tensor_tensor(dst[:, PADS:], src[:, PADS:], src[:, PADS - k:384 - k], ALU.add))
                src, dst = dst, src
            F, rise = src[:, PADS:], dst[:, PADS:]
            then(nc.gpsimd.tensor_tensor(iT, iT, F, ALU.subtract))
            then(nc.gpsimd.tensor_scalar(g0[:, PADS:], iT, 0.0, None, ALU.max))
            src, dst = g0, g1
            for k in (1, 2, 4, 8, 16, 32, 64, 128):
                then(nc.gpsimd.tensor_tensor(rise, src[:, PADS - k:384 - k], src[:, PADS:], ALU.subtract))
                then(nc.gpsimd.tensor_scalar(rise, rise, 0.0, None, ALU.max))
                then(nc.gpsimd.tensor_tensor(dst[:, PADS:], src[:, PADS:], rise, ALU.add))
                src, dst = dst, src
            then(nc.gpsimd.tensor_tensor(F, F, src[:, PADS:], ALU.add))
            then(nc.gpsimd.tensor_scalar(F, F, -40.0, None, ALU.max))
            then(nc.gpsimd.tensor_scalar(src[:, PADS:], src[:, PADS:], -1.0, None, ALU.mult))
            for row, val in enumerate((src[:, PADS:], iT, F)):
                pool.dma_start(rows_dram[row], val).then_inc(gate_io2, 16)
            pool.wait_ge(gate_io2, 48)
            pool.dma_start(neg_g[:].rearrange("p h t -> p (h t)"),
                           rows_dram[0].rearrange("h t -> (h t)").partition_broadcast(P)).then_inc(gates_ready, 16)
            with nc.allow_non_contiguous_dma("gates by token, a few thousand elements"):
                for which in range(2):
                    for b in range(TB):
                        pool.dma_start(um[:, which, b, :], rows_dram[1 + which][:, b * P:(b + 1) * P].rearrange("h p -> p h")
                                       ).then_inc(gates_ready, 16)

            with pool.Fori(0, TURNS_MIX) as g:
                pool.wait_ge(a_ss, g + 1)
                root(ss[:, 4:8], ss[:, 0:4], 1).then_inc(a_rs, 1)
                pool.wait_ge(m_d2, g + 1)
                pool.wait_ge(m_ss, g + 1)
                den = den2[:].rearrange("p j b -> p (j b)")
                nc.gpsimd.tensor_tensor(den, den, terms[:, 1, :], ALU.mult)
                pool.drain()
                nc.gpsimd.tensor_tensor(ss[:, 8:12], ss[:, 8:12], den, ALU.add)
                pool.drain()
                root(ss[:, 12:16], ss[:, 8:12], 2).then_inc(m_rs, 1)

            for b in range(TB):
                inverse_root(S_MS + 2 * b, ms_half, 2 * b + 2, S_RS + b, mix_rs)
                inverse_root(X_MS + 2 * b, x_ms, 2 * TB + 2 * b + 2, X_RS + b, x_rs)
            for b in range(TB):
                inverse_root(S_MS + 2 * b, ms_half, 2 * TB + 2 * b + 2, S_RS + b, mix_rs)

        @block.scalar
        def _(scalar):
            def copy(out_ap, in_ap, scale=1.0):
                return nc.scalar.activation(out_ap, in_ap, ACT.Copy, scale=scale)

            def split(n4, n, slot):
                scalar.wait_ge(raw_loaded[slot], n4 * 16 + 16)
                scalar.wait_ge(pe_done, n + 1)
                copy(w_hi[:, slot, :], raw[:, slot, :]).then_inc(hi_done, 1)

            def split_ahead(turn, per_turn, base, u):
                u += LOOKAHEAD
                split(turn * (per_turn // RING) + (base + u) // RING, turn * per_turn + (base + u), u % RING)

            def banks(lo, n, k):
                return ps[:, lo:lo + n, :].rearrange("p b (t c) -> p (b t) c", c=k)

            def norm_tiles(count, gain, before={}):
                for k in range(KT):
                    if k in before:
                        before[k]()
                    if k % 2 == 0:
                        scalar.wait_ge(h_psum, (count + k) // 2 + 1)
                    ins = copy(h_hi[:, k, :], ps[:, tile_bank(k), k % 2 * T:k % 2 * T + T],
                               scale=chan[:, gain + k:gain + k + 1])
                    if k % 2:
                        ins.then_inc(h_hi_done, 1)

            def squares_out(n, tensor=act):
                return tensor[:, 4 * n:4 * n + 4, :].rearrange("p t c -> p (t c)")

            def square_half(src, junk, column, done):
                nc.scalar.activation(junk, src, ACT.Square, scale=float(D) ** -0.5,
                                     accum_out=stat[:, column:column + 1]).then_inc(done, 1)

            nc.scalar.sem_inc(read_act, 2)
            nc.scalar.sem_inc(ga_read, 1)
            scalar.dma_start(shp[:], consts).then_inc(shp_loaded, 16)

            for b in range(TB):
                for h in range(2):
                    scalar.wait_ge(x_loaded[2 * b + h], 16)
                    square_half(half_of(gm_rows, b, h), squares_out(2 * b + h, ha_hi), X_MS + 2 * b + h, x_ms)
            lams = on[:].rearrange("p a b c -> p (a b c)")
            scalar.dma_start(lams[:, 0:4 * QKD], lambdas.partition_broadcast(P)).then_inc(lam_loaded, 16)
            scalar.wait_ge(chanT, 1)
            copy(chan[:, 0:401], ps[:, 0, 0:401])
            copy(chan[:, 401:577], ps[:, 1, 0:176]).then_inc(chan_raw, 1)
            scalar.wait_ge(wif_loaded, 16)
            scalar.wait_ge(wif_zero, 1)
            copy(hm_hi[:, :, 0:HEADS], wif_raw[:, :, 0:HEADS])
            copy(hm_hi[:, :, F_ROW:F_ROW + HEADS], wif_raw[:, :, HEADS:]).then_inc(wif_h, 1)
            scalar.wait_ge(chan_ready, 1)
            norm_tiles(0, C_GPM, {12: lambda: split(0, 0, 0)})
            for u in range(1, LOOKAHEAD):
                split(0, u, u)
            scalar.wait_ge(gates_psum, 1)
            nc.scalar.activation(iT, ps[0:HEADS, 7, 0:T], ACT.Identity, bias=chan[0:HEADS, C_GB:C_GB + 1])
            nc.scalar.activation(fT, ps[F_ROW:F_ROW + HEADS, 7, 0:T], ACT.Identity,
                                 bias=chan[F_ROW:F_ROW + HEADS, C_GB:C_GB + 1]).then_inc(gates_sb, 1)
            scalar.drain()
            nc.scalar.activation(gate_log, fT, ACT.Abs)
            scalar.drain()
            nc.scalar.activation(gate_log, gate_log, ACT.Exp, scale=-1.0)
            scalar.drain()
            nc.scalar.activation(gate_log, gate_log, ACT.Ln, bias=1.0).then_inc(gates_log, 1)
            scalar.wait_ge(lam_dots, 1)
            nc.scalar.activation(lam[:, 0:2], lam[:, 0:2], ACT.Exp).then_inc(lam_exp, 1)

            def conv_terms(g, c, pair, dst, tiles):
                for t in tiles:
                    tile = g * 4 + (t + (KT if c == 4 else 0))
                    nc_in = ps[:, 2 * pair + t // 2, t % 2 * T:t % 2 * T + T]
                    ins = nc.scalar.activation(dst[:, t, :], nc_in, ACT.Identity, bias=chan[:, ds(tile + C_MCB, 1)],
                                               scale=chan[:, ds(tile + (C_MCW + 96), 1)])
                ins.then_inc(conv_bias, 1)

            with scalar.Fori(0, TURNS_MIX) as g:
                for u in range(U_MIX):
                    split_ahead(g, U_MIX, BASE_MIX, u)
                    if u == 7:
                        scalar.wait_ge(pe_done, g * U_MIX + units_done(u))
                        copy(qT[:], banks(0, 2, T)).then_inc(read_act, 1)
                    if u == 15:
                        scalar.wait_ge(pe_done, g * U_MIX + units_done(u))
                        copy(kT[:], banks(2, 2, T)).then_inc(read_act, 1)
                    if u == 23:
                        scalar.wait_ge(pe_done, g * U_MIX + units_done(u))
                        copy(v[:], banks(0, 2, 512)).then_inc(read_act, 1)
                    if u in (20, 22):
                        j = (u - 20) // 2
                        scalar.wait_ge(a_max, g * 2 + (j + 1))
                        for m in range(2):
                            for blk, (c0, c1) in enumerate(((0, 128), (128, 384))):
                                ins = nc.scalar.activation(prob[:, 2 * j + m, c0:c1], prob[:, 2 * j + m, c0:c1], ACT.Exp,
                                                           bias=mx[:, j, blk, m:m + 1], scale=SCALE_A,
                                                           accum_out=sm[:, j, blk, m:m + 1])
                        ins.then_inc(a_exp, 1)
                    if u == 25:
                        scalar.wait_ge(a_probT, g + 1)
                        copy(attnT[:], ps[:, 4:6, 0:384]).then_inc(a_probT_sb, 1)
                    if u == 28:
                        scalar.wait_ge(a_num, g + 1)
                        for j in range(2):
                            for b in range(TB):
                                ins = nc.scalar.activation(on[:, b, j, :], ps[:, 6 + j, b * HD:b * HD + HD], ACT.Square,
                                                           scale=float(HD) ** -0.5, accum_out=ss[:, 2 * j + b:2 * j + b + 1])
                        ins.then_inc(a_ss, 1)
                    if u == 37:
                        scalar.wait_ge(a_onT, g + 1)
                        for t in range(4):
                            ins = nc.scalar.activation(ha_hi[:, ds(g * 4 + t, 1), :],
                                                       ps[:, 4 + t // 2:5 + t // 2, t % 2 * T:t % 2 * T + T], ACT.Copy,
                                                       scale=chan[:, ds(g * 4 + (C_GAH + t), 1)])
                        ins.then_inc(a_hi, 1)
                    if u in (31, 32, 39, 40):
                        c = 3 if u < 35 else 4
                        dst = qT if c == 3 else kT
                        t0 = 0 if u % 8 == 7 else 2
                        if t0 == 0:
                            scalar.wait_ge(pe_done, g * U_MIX + units_done(u))
                        conv_terms(g, c, c % 2, dst, (t0, t0 + 1))
                    if u in (34, 42):
                        dst = qT if u == 34 else kT
                        scalar.wait_ge(conv_sum, g * 4 + (2 if u == 34 else 4))
                        nc.scalar.activation(prob[:].rearrange("p a b -> p (a b)")[:, 0:4 * T],
                                             dst[:].rearrange("p t c -> p (t c)"), ACT.Tanh, scale=0.5).then_inc(conv_tanh, 1)
                    if u == 44:
                        scalar.wait_ge(m_arg, g + 1)
                        for j in range(2):
                            for b, (c0, c1) in enumerate(((0, 256), (256, 384))):
                                ins = nc.scalar.activation(prob[:, j, c0:c1], prob[:, j, c0:c1], ACT.Exp,
                                                           bias=um[:, 0, b, ds(g * 2 + j, 1)])
                        ins.then_inc(m_w, 1)
                    if u == 47:
                        scalar.wait_ge(pe_done, g * U_MIX + units_done(u))
                        copy(v[:], banks(2, 2, 512)).then_inc(read_act, 1)
                    if u == 51:
                        scalar.wait_ge(m_num, g + 1)
                        for j in range(2):
                            for b in range(TB):
                                ins = nc.scalar.activation(on[:, b, j, :], ps[:, 6 + j, b * HD:b * HD + HD], ACT.Square,
                                                           scale=float(HD) ** -0.5, accum_out=ss[:, 8 + 2 * j + b:9 + 2 * j + b])
                        nc.scalar.activation(floor2[:], um[:, 1, :, ds(g * 2, 2)].rearrange("p b j -> p j b"), ACT.Exp,
                                             scale=-2.0).then_inc(m_ss, 1)
                    if u == 55:
                        scalar.wait_ge(pe_done, g * U_MIX + units_done(u))
                        nc.scalar.activation(og[:], banks(0, 2, T), ACT.Tanh, scale=0.5).then_inc(read_act, 1)
                    if u == 59:
                        scalar.wait_ge(m_gated, g + 2)
                        tmp = prob[:].rearrange("p a b -> p (a b)")[:, 0:4 * T].rearrange("p (t c) -> p t c", c=T)
                        for t in range(4):
                            ins = nc.scalar.activation(hm_hi[:, ds(g * 4 + t, 1), :], tmp[:, t:t + 1, :], ACT.Copy,
                                                       scale=chan[:, ds(g * 4 + (C_GMH + t), 1)])
                        ins.then_inc(m_hi, 1)
                    if u == 63:
                        scalar.wait_ge(pe_done, g * U_MIX + units_done(u))
                        nc.scalar.activation(gm[:, ds(g * 4, 4), :], banks(2, 2, T), ACT.Tanh, scale=0.5).then_inc(read_act, 1)

            with scalar.Fori(0, TURNS_BR) as g:
                for u in range(U_BR):
                    split_ahead(g, U_BR, BASE_BR, u)
                    if u == 7:
                        scalar.wait_ge(pe_done, g * U_BR + units_done(BASE_BR + u))
                        scalar.wait_ge(y_ready, g + 1)
                        nc.scalar.activation(ga[:], banks(4, 2, T), ACT.Tanh, scale=0.5).then_inc(ga_read, 1)

            def split_last(first_unit, u):
                n = first_unit + u
                scalar.wait_ge(raw_loaded[u % RING], n // RING * 16 + 16)
                if u < RING:
                    scalar.wait_ge(pe_done, n + 1)
                copy(last_split(u)[0], raw[:, u % RING, :]).then_inc(hi_done, 1)

            def rows_phase(turns, per_turn, base, src, scale, src_ready, then_load, rest=None):
                for k in range(RING):
                    copy(ks_hi[:, k:k + 1, :], src[:, k:k + 1, :], scale=scale).then_inc(ks_h, 1)
                if rest:
                    rest()

                def turn(g, first, last):
                    for u in range(per_turn):
                        if not last:
                            split_ahead(g, per_turn, base, u)
                        elif u + LOOKAHEAD < per_turn:
                            split_last(g * per_turn + base, u + LOOKAHEAD)
                        if first and u == 5:
                            scalar.wait_ge(*src_ready)
                            then_load()
                        k = next_tile(u, first, last)
                        if k:
                            copy(ks_hi[:, k % RING:k % RING + 1, :], src[:, ds(g * 4 + k, 1), :], scale=scale).then_inc(ks_h, 1)

                turn(0, True, False)
                with scalar.Fori(1, turns - 1) as g:
                    turn(g, False, False)
                turn(turns - 1, False, True)

            def load_residual():
                scalar.dma_start(x1[:], x_v).then_inc(xres_loaded, 16)
                scalar.dma_start(gpost[:, 0, :], g_post_mix[0].partition_broadcast(P)).then_inc(gpost_loaded, 16)

            scalar.wait_ge(y_ready, 2)
            rows_phase(TURNS_OUT, U_OUT, BASE_OUT, y, 0.5, (y_ready, TURNS_BR + 1), load_residual)

            def output_squares(b, h, count, last_unit):
                if b == 0:
                    scalar.wait_ge(half_done, count + h + 1)
                else:
                    scalar.wait_ge(pe_done, units_done(last_unit if h else last_unit - RING))
                square_half(ps_half(b, h), squares_out(2 * b + h), S_MS + 2 * b + h, ms_half)

            def residual_squares(b, h):
                scalar.wait_ge(x1_ready, 2 * b + h + 1)
                square_half(half_of(x1, b, h), squares_out(4 + 2 * b + h), X_MS + 2 * b + h, x_ms)

            output_squares(0, 0, 0, BASE_UP - 1)
            output_squares(0, 1, 0, BASE_UP - 1)
            residual_squares(0, 0)
            residual_squares(0, 1)
            output_squares(1, 0, 0, BASE_UP - 1)
            for u in range(LOOKAHEAD):
                scalar.wait_ge(raw_loaded[u], BASE_UP // RING * 16 + 16)
                copy(w_hi[:, u, :], raw[:, u, :]).then_inc(hi_done, 1)
            output_squares(1, 1, 0, BASE_UP - 1)
            residual_squares(1, 0)
            residual_squares(1, 1)
            norm_tiles(KT, C_GPF)

            def up_terms(g, first_tile, pair, dst):
                for t in range(4):
                    tile = g * 4 + (first_tile + t)
                    ins = nc.scalar.activation(dst[:, t, :], ps[:, 2 * pair + t // 2, t % 2 * T:t % 2 * T + T], ACT.Identity,
                                               bias=chan[:, ds(tile + C_FCB, 1)], scale=chan[:, ds(tile + (C_FCW + 176), 1)])
                    if t % 2:
                        ins.then_inc(up_bias, 1)

            def value_terms(g):
                scalar.wait_ge(pe_done, g * U_UP + units_done(BASE_UP + U_UP - 1))
                up_terms(g, FT, 1, gate[:, 4:8, :])

            def up_turn(g, first):
                for u in range(U_UP):
                    split_ahead(g, U_UP, BASE_UP, u)
                    if u == 0 and not first:
                        value_terms(g - 1)
                    if u == 7:
                        scalar.wait_ge(pe_done, g * U_UP + units_done(BASE_UP + u))
                        scalar.wait_ge(act_ready, g + 1)
                        up_terms(g, 0, 0, gate)
                    if u == 10:
                        scalar.wait_ge(gate_read, g * 2 + 3)
                        nc.scalar.activation(poly[:, 0:4, :], gate[:, 0:4, :], ACT.Square).then_inc(gate_sq, 1)
                    if u == 12:
                        scalar.wait_ge(gate_arg, g + 1)
                        nc.scalar.activation(poly[:, 0:4, :], poly[:, 0:4, :], ACT.Tanh,
                                             scale=(2.0 / np.pi) ** 0.5).then_inc(gate_tanh, 1)

            up_turn(0, True)
            with scalar.Fori(1, TURNS_UP) as g:
                up_turn(g, False)

            def load_gain():
                scalar.dma_start(gpost[:, 0, :], g_post_ffn[0].partition_broadcast(P)).then_inc(gpost_loaded, 16)

            rows_phase(TURNS_DOWN, U_DOWN, BASE_DOWN, act, 1.0, (act_ready, TURNS_UP + 1), load_gain,
                       lambda: value_terms(TURNS_UP - 1))
            for b in range(TB):
                for h in range(2):
                    output_squares(b, h, TB, UNITS - 1)

        @block.vector
        def _(vec):
            def stt(out_ap, in0, scalar, in1, op0, op1):
                return nc.vector.scalar_tensor_tensor(out=out_ap, in0=in0, scalar=scalar, in1=in1, op0=op0, op1=op1)

            def split(n, slot):
                vec.wait_ge(hi_done, n + 1)
                nc.vector.tensor_tensor(w_lo[:, slot, :], raw[:, slot, :], w_hi[:, slot, :].bitcast(F32),
                                        ALU.subtract).then_inc(lo_done, 1)

            def split_ahead(turn, per_turn, base, u):
                u += LOOKAHEAD
                split(turn * per_turn + (base + u), u % RING)

            def norm_tiles(count, gain, before):
                for k in range(KT):
                    if k in before:
                        before[k]()
                    if k % 2 == 0:
                        vec.wait_ge(h_hi_done, (count + k) // 2 + 1)
                    stt(h_lo[:, k, :], ps[:, tile_bank(k), k % 2 * T:k % 2 * T + T], chan[:, gain + k:gain + k + 1],
                        h_hi[:, k, :].bitcast(F32), ALU.mult, ALU.subtract).then_inc(h_done, 1)

            nc.vector.sem_inc(raw_free, RING)
            for starts_at_one in (m_gated, y_ready, bm_read, ba_read, gate_read, val_read, act_ready):
                nc.vector.sem_inc(starts_at_one, 1)

            def normed(b, dst, src, count):
                vec.wait_ge(x_rs, count + b + 1)
                for h in range(2):
                    nc.vector.tensor_scalar(half_of(dst, b, h), half_of(src, b, h), stat[:, X_RS + b:X_RS + b + 1], None,
                                            ALU.mult).then_inc(xn_ready, 1)

            normed(0, gm_rows, gm_rows, 0)
            normed(1, gm_rows, gm_rows, 0)
            vec.wait_ge(chan_raw, 1)
            nc.vector.tensor_scalar(chan[:, C_GMH:C_GMH + KT], chan[:, C_GMH:C_GMH + KT], 0.5, None, ALU.mult)
            nc.vector.tensor_scalar(chan[:, C_GAH:C_GAH + KT], chan[:, C_GAH:C_GAH + KT], 1.0 - LAM_INIT, None,
                                    ALU.mult).then_inc(chan_ready, 1)
            vec.wait_ge(wif_h, 1)
            for col, c0 in ((0, 0), (F_ROW, HEADS)):
                ins = nc.vector.tensor_tensor(hm_lo[:, :, col:col + HEADS], wif_raw[:, :, c0:c0 + HEADS],
                                              hm_hi[:, :, col:col + HEADS].bitcast(F32), ALU.subtract)
            ins.then_inc(wif_ready, 1)
            norm_tiles(0, C_GPM, {12: lambda: split(0, 0)})
            for u in range(1, LOOKAHEAD):
                split(u, u)
            vec.wait_ge(lam_loaded, 16)
            lams = on[:].rearrange("p a b c -> p (a b c)")
            nc.vector.tensor_tensor(lams[:, 512:768], lams[:, 0:256], lams[:, 256:512], ALU.mult)
            vec.drain()
            nc.vector.reduce_sum(lam[:, 0:2], lams[:, 512:768].rearrange("p (a c) -> p a c", a=2), AX_X).then_inc(lam_dots, 1)
            vec.wait_ge(lam_exp, 1)
            stt(lam[:, 2:3], lam[:, 1:2], -LAM_INIT, lam[:, 0:1], ALU.add, ALU.subtract)
            vec.drain()

            alibi = shp[:, S_ALIBI:S_ALIBI + 384].unsqueeze(1).broadcast_to([P, 2, 384])
            tri = shp[:, S_TRI:S_TRI + P].unsqueeze(1).broadcast_to([P, 2, P])
            flat = prob[:].rearrange("p a b -> p (a b)")

            def conv_taps(g, c, pair, dst, tiles, taps, first_tile, weight, stride):
                for j in range(1, taps):
                    for t in tiles:
                        tile = g * 4 + (first_tile + t)
                        off = t % 2 * T
                        ins = stt(dst[:, t, j:], ps[:, 2 * pair + t // 2, off:off + T - j],
                                  chan[:, ds(tile + (weight + (taps - 1 - j) * stride), 1)], dst[:, t, j:], ALU.mult, ALU.add)
                    if j < taps - 1:
                        vec.drain()
                return ins

            with vec.Fori(0, TURNS_MIX) as g:
                for u in range(U_MIX):
                    split_ahead(g, U_MIX, BASE_MIX, u)
                    if u in (18, 20):
                        j = (u - 18) // 2
                        vec.wait_ge(a_score, g * 2 + (j + 1))
                        stt(prob[:, 2 * j:2 * j + 2, :], alibi, shp[:, ds(g * 2 + (S_SLOPE + j), 1)],
                            ps[:, 4 + 2 * j:6 + 2 * j, 0:384], ALU.mult, ALU.add)
                        vec.drain()
                        nc.vector.reduce_max(mx[:, j, 0, :], prob[:, 2 * j:2 * j + 2, 0:128], AX_X)
                        nc.vector.reduce_max(mx[:, j, 1, :], prob[:, 2 * j:2 * j + 2, 128:384], AX_X)
                        vec.drain()
                        nc.vector.tensor_scalar(mx[:, j, :, :], mx[:, j, :, :], -SCALE_A, None, ALU.mult).then_inc(a_max, 1)
                    if u in (21, 23):
                        j = (u - 21) // 2
                        vec.wait_ge(a_exp, g * 2 + (j + 1))
                        nc.vector.reciprocal(sm[:, j, :, :], sm[:, j, :, :])
                        vec.drain()
                        nc.vector.tensor_scalar(sm[:, j, :, 1:2], sm[:, j, :, 1:2], lam[:, 2:3], None, ALU.mult)
                        for blk, (c0, c1) in enumerate(((0, 128), (128, 384))):
                            nc.vector.tensor_scalar(prob[:, 2 * j, c0:c1], prob[:, 2 * j, c0:c1], sm[:, j, blk, 0:1], None, ALU.mult)
                        vec.drain()
                        for blk, (c0, c1) in enumerate(((0, 128), (128, 384))):
                            ins = stt(prob[:, 2 * j, c0:c1], prob[:, 2 * j + 1, c0:c1], sm[:, j, blk, 1:2],
                                      prob[:, 2 * j, c0:c1], ALU.mult, ALU.add)
                        ins.then_inc(a_prob, 1)
                    if u == 29:
                        vec.wait_ge(a_rs, g + 1)
                        for j in range(2):
                            for b in range(TB):
                                ins = nc.vector.tensor_scalar(on[:, b, j, :], ps[:, 6 + j, b * HD:b * HD + HD],
                                                              ss[:, 4 + 2 * j + b:5 + 2 * j + b], None, ALU.mult)
                        ins.then_inc(a_on, 1)
                    if u == 38:
                        vec.wait_ge(a_hi, g + 1)
                        for t in range(4):
                            ins = stt(ha_lo[:, ds(g * 4 + t, 1), :], ps[:, 4 + t // 2:5 + t // 2, t % 2 * T:t % 2 * T + T],
                                      chan[:, ds(g * 4 + (C_GAH + t), 1)], ha_hi[:, ds(g * 4 + t, 1), :].bitcast(F32),
                                      ALU.mult, ALU.subtract)
                        ins.then_inc(a_done, 1)
                    if u in (31, 33, 39, 41):
                        c = 3 if u < 35 else 4
                        t0 = 0 if u % 8 == 7 else 2
                        vec.wait_ge(conv_bias, g * 4 + ((c - 3) * 2 + t0 // 2 + 1))
                        ins = conv_taps(g, c, c % 2, qT if c == 3 else kT, (t0, t0 + 1), 4, (c - 3) * KT, C_MCW, 32)
                        ins.then_inc(conv_sum, 1)
                        if t0 == 2:
                            vec.drain().then_inc(read_dve, 1)
                    if u in (35, 43):
                        dst = (qT if u == 35 else kT)[:].rearrange("p t c -> p (t c)")
                        vec.wait_ge(conv_tanh, g * 2 + (1 if u == 35 else 2))
                        stt(dst, flat[:, 0:4 * T], 1.0, dst, ALU.add, ALU.mult).then_inc(qk_ready, 1)
                    if u == 43:
                        vec.drain()
                        vec.wait_ge(gates_ready, 80)
                        for j in range(2):
                            row = neg_g[:, ds(g * 2 + j, 1), :]
                            w3 = prob[:, j, :].rearrange("p (b c) -> p b c", c=P)
                            nc.vector.tensor_tensor(w3[:, 0:3:2, :], row.rearrange("p a (b c) -> p (a b) c", c=P), tri, ALU.add)
                            ins = nc.vector.tensor_copy(prob[:, j:j + 1, P:2 * P], row[:, :, P:2 * P])
                        ins.then_inc(m_arg, 1)
                    if u == 46:
                        vec.wait_ge(m_w, g + 1)
                        vec.wait_ge(m_score, g + 1)
                        for j in range(2):
                            ins = stt(prob[:, 2 + j, :], ps[:, 4 + j, 0:384], 0.25 * float(HD) ** -0.5, prob[:, j, :],
                                      ALU.mult, ALU.mult)
                        ins.then_inc(m_at, 1)
                    if u == 51:
                        vec.wait_ge(m_num, g + 1)
                        nc.vector.tensor_copy(den2[:], ps[:, 4:6, 384:386])
                        vec.drain()
                        nc.vector.tensor_tensor(den2[:], den2[:], den2[:], ALU.mult)
                        vec.drain()
                        vec.wait_ge(m_ss, g + 1)
                        nc.vector.tensor_tensor(den2[:], den2[:], floor2[:], ALU.max).then_inc(m_d2, 1)
                    if u == 53:
                        vec.wait_ge(m_rs, g + 1)
                        for j in range(2):
                            for b in range(TB):
                                ins = nc.vector.tensor_scalar(on[:, b, j, :], ps[:, 6 + j, b * HD:b * HD + HD],
                                                              ss[:, 12 + 2 * j + b:13 + 2 * j + b], None, ALU.mult)
                        ins.then_inc(m_on, 1)
                    if u == 59:
                        vec.wait_ge(m_onT, g + 1)
                        vec.wait_ge(read_act, g * 6 + 7)
                        stt(flat[:, 0:4 * T].rearrange("p (a b) -> p a b", a=2), og[:].rearrange("p (a t) c -> p a (t c)", a=2),
                            1.0, ps[:, 4:6, :], ALU.add, ALU.mult).then_inc(m_gated, 1)
                    if u == 60:
                        vec.wait_ge(m_hi, g + 1)
                        tmp = flat[:, 0:4 * T].rearrange("p (t c) -> p t c", c=T)
                        for t in range(4):
                            ins = stt(hm_lo[:, ds(g * 4 + t, 1), :], tmp[:, t:t + 1, :], chan[:, ds(g * 4 + (C_GMH + t), 1)],
                                      hm_hi[:, ds(g * 4 + t, 1), :].bitcast(F32), ALU.mult, ALU.subtract)
                        ins.then_inc(m_done, 1)

            def halves(ap):
                return ap.rearrange("p (a t) c -> p a (t c)", a=2)

            def branch_sum(g):
                vec.wait_ge(pe_done, g * U_BR + units_done(BASE_BR + U_BR - 1))
                vec.wait_ge(ga_read, g + 2)
                stt(halves(y_tmp[:]), halves(ga[:]), 1.0, ps[:, 2:4, :], ALU.add, ALU.mult).then_inc(ba_read, 1)
                vec.drain()
                nc.vector.tensor_tensor(y[:, ds(g * 4, 4), :], y[:, ds(g * 4, 4), :], y_tmp[:], ALU.add).then_inc(y_ready, 1)

            def branch_turn(g, last):
                for u in range(U_BR):
                    split_ahead(g, U_BR, BASE_BR, u)
                    if u == 15:
                        vec.wait_ge(pe_done, g * U_BR + units_done(BASE_BR + u))
                        vec.wait_ge(read_act, 6 * TURNS_MIX + 2)
                        stt(halves(y[:, ds(g * 4, 4), :]), halves(gm[:, ds(g * 4, 4), :]), 1.0, ps[:, 0:2, :],
                            ALU.add, ALU.mult).then_inc(bm_read, 1)
                    if u == 23 and not last:
                        branch_sum(g)

            with vec.Fori(0, TURNS_BR - 1) as g:
                branch_turn(g, False)
            branch_turn(TURNS_BR - 1, True)

            def split_last(first_unit, u):
                vec.wait_ge(hi_done, first_unit + u + 1)
                hi, lo = last_split(u)
                nc.vector.tensor_tensor(lo, raw[:, u % RING, :], hi.bitcast(F32), ALU.subtract).then_inc(lo_done, 1)

            def rows_phase(turns, per_turn, base, src, scale, tiles_before, rest, late_rest=None):
                def lo(k, slot, count):
                    vec.wait_ge(ks_h, count)
                    stt(ks_lo[:, slot:slot + 1, :], src[:, k, :], scale, ks_hi[:, slot:slot + 1, :].bitcast(F32),
                        ALU.mult, ALU.subtract).then_inc(ks_done, 1)

                for k in range(RING):
                    lo(slice(k, k + 1), k, tiles_before + k + 1)
                rest()

                def turn(g, first, last):
                    for u in range(per_turn):
                        if not last:
                            split_ahead(g, per_turn, base, u)
                        elif u + LOOKAHEAD < per_turn:
                            split_last(g * per_turn + base, u + LOOKAHEAD)
                        if first and u == 1 and late_rest:
                            late_rest()
                        k = next_tile(u, first, last)
                        if k:
                            lo(ds(g * 4 + k, 1), k % RING, g * 4 + (tiles_before + k + 1))

                turn(0, True, False)
                with vec.Fori(1, turns - 1) as g:
                    turn(g, False, False)
                turn(turns - 1, False, True)

            rows_phase(TURNS_OUT, U_OUT, BASE_OUT, y, 0.5, 0, lambda: branch_sum(TURNS_BR - 1))

            def gain_half(b, h, count):
                vec.wait_ge(ms_half, 2 * (count + b) + h + 1)
                nc.vector.tensor_tensor(half_of(xn, b, h), ps_half(b, h), half_of(gpost, 0, h), ALU.mult).then_inc(gained, 1)

            def residual(b, count, dst, done):
                vec.drain()
                vec.wait_ge(mix_rs, count + b + 1)
                for h in range(2):
                    stt(half_of(dst, b, h), half_of(xn, b, h), stat[:, S_RS + b:S_RS + b + 1], half_of(x1, b, h),
                        ALU.mult, ALU.add).then_inc(done, 1)

            vec.wait_ge(gpost_loaded, 16)
            vec.wait_ge(xres_loaded, 16)
            gain_half(0, 0, 0)
            gain_half(0, 1, 0)
            residual(0, 0, x1, x1_ready)
            gain_half(1, 0, 0)
            normed(0, xn, x1, TB)
            split(BASE_UP, 0)
            gain_half(1, 1, 0)
            residual(1, 0, x1, x1_ready)
            split(BASE_UP + 1, 1)
            normed(1, xn, x1, TB)
            norm_tiles(KT, C_GPF, {8: lambda: split(BASE_UP + 2, 2)})

            def value_head(g):
                vec.wait_ge(up_bias, g * 4 + 3)
                conv_taps(g, 1, 1, gate[:, 4:8, :], (0, 1), 3, FT, C_FCW, 88)

            def value_tail(g):
                vec.wait_ge(up_bias, g * 4 + 4)
                conv_taps(g, 1, 1, gate[:, 4:8, :], (2, 3), 3, FT, C_FCW, 88).then_inc(val_read, 1)
                vec.drain()
                stt(act[:, ds(g * 4, 4), :], gate[:, 0:4, :], 0.5, gate[:, 4:8, :], ALU.mult, ALU.mult).then_inc(act_ready, 1)

            def up_turn(g, first):
                for u in range(U_UP):
                    split_ahead(g, U_UP, BASE_UP, u)
                    if u == 0 and not first:
                        value_head(g - 1)
                    if u == 2 and not first:
                        value_tail(g - 1)
                    if u in (7, 9):
                        i = (u - 7) // 2
                        vec.wait_ge(up_bias, g * 4 + (i + 1))
                        conv_taps(g, 0, 0, gate, (2 * i, 2 * i + 1), 3, 0, C_FCW, 88).then_inc(gate_read, 1)
                    if u == 11:
                        vec.wait_ge(gate_sq, g + 1)
                        nc.vector.tensor_scalar(poly[:, 0:4, :], poly[:, 0:4, :], 0.044715, 1.0, ALU.mult, ALU.add)
                        vec.drain()
                        nc.vector.tensor_tensor(poly[:, 0:4, :], poly[:, 0:4, :], gate[:, 0:4, :], ALU.mult).then_inc(gate_arg, 1)
                    if u == 13:
                        vec.wait_ge(gate_tanh, g + 1)
                        stt(gate[:, 0:4, :], poly[:, 0:4, :], 1.0, gate[:, 0:4, :], ALU.add, ALU.mult)

            up_turn(0, True)
            with vec.Fori(1, TURNS_UP) as g:
                up_turn(g, False)
            rows_phase(TURNS_DOWN, U_DOWN, BASE_DOWN, act, 1.0, KT, lambda: value_head(TURNS_UP - 1),
                       lambda: value_tail(TURNS_UP - 1))
            vec.wait_ge(gpost_loaded, 32)
            for b in range(TB):
                for h in range(2):
                    gain_half(b, h, TB)
                residual(b, TB, xn, fin_ready)

        @block.tensor
        def _(pe):
            def three(out_ap, stat_hi, stat_lo, mov_hi, mov_lo, start, stop):
                nc.tensor.matmul(out_ap, stat_hi, mov_hi, start=start, stop=False, skip_group_check=True)
                nc.tensor.matmul(out_ap, stat_hi, mov_lo, start=False, stop=False, skip_group_check=True)
                return nc.tensor.matmul(out_ap, stat_lo, mov_hi, start=False, stop=stop, skip_group_check=True)

            def ready(n):
                pe.wait_ge(lo_done, n + 1 + RING)

            def unit_channels(u, pair, a_hi_t, a_lo_t):
                slot = u % RING
                for kk in range(2):
                    k = 2 * (u % UNITS_CHUNK) + kk
                    for t in range(4):
                        c = kk * 512 + t * P
                        last = three(ps[:, 2 * pair + t // 2, t % 2 * T:t % 2 * T + T],
                                     w_hi[:, slot, c:c + P], w_lo[:, slot, c:c + P], a_hi_t[:, k, :], a_lo_t[:, k, :],
                                     start=k == 0 and t % 2 == 0, stop=k == KT - 1)
                last.then_inc(pe_done, 1)

            def unit_tokens(u, pair):
                slot = u % RING
                for kk in range(2):
                    k = 2 * (u % UNITS_CHUNK) + kk
                    for b in range(TB):
                        last = three(ps[:, 2 * pair + b, :], h_hi[:, k, b * P:(b + 1) * P], h_lo[:, k, b * P:(b + 1) * P],
                                     w_hi[:, slot, kk * 512:kk * 512 + 512], w_lo[:, slot, kk * 512:kk * 512 + 512],
                                     start=k == 0, stop=k == KT - 1)
                last.then_inc(pe_done, 1)

            def transposes(src, count):
                EARLY = 10
                ready = count // KT * 2 * TB

                def tile(k, b):
                    return nc.tensor.transpose(ps[:, tile_bank(k), k % 2 * T + b * P:k % 2 * T + (b + 1) * P],
                                               src[:, b, k * P:(k + 1) * P], ident)

                for k in range(EARLY):
                    if k % (KT // 2) == 0:
                        pe.wait_ge(xn_ready, ready + k // (KT // 2) + 1)
                    if count and k in (4, 8):
                        pe.wait_ge(gained, 3 if k == 4 else 4)
                    tile(k, 0)
                for k in range(KT):
                    if k % 2 == 0 and k >= EARLY:
                        pe.wait_ge(h_done, count + k - EARLY + 2)
                    if k % (KT // 2) == 0:
                        pe.wait_ge(xn_ready, ready + k // (KT // 2) + 3)
                    if k >= EARLY:
                        tile(k, 0)
                    last = tile(k, 1)
                    if k % 2:
                        last.then_inc(h_psum, 1)

            def head_values(weights, j):
                for b, parts in ((0, ((0, 0),)), (1, ((1, 0), (2, 1)))):
                    for i, (part, s) in enumerate(parts):
                        last = nc.tensor.matmul(ps[:, 6 + j, b * HD:(b + 1) * HD], weights[:, part * P:(part + 1) * P],
                                                v[:, s, j * HD:(j + 1) * HD], start=i == 0, stop=i == len(parts) - 1)
                return last

            def heads_out():
                for t in range(4):
                    for b in range(TB):
                        last = nc.tensor.transpose(ps[:, 4 + t // 2, t % 2 * T + b * P:t % 2 * T + (b + 1) * P],
                                                   on[:, b, t // 2, t % 2 * P:(t % 2 + 1) * P], ident)
                return last

            nc.tensor.sem_inc(pe_done, RING)
            pe.wait_ge(shp_loaded, 16)
            pe.wait_ge(rows_loaded, 16 * 3)
            for k, (rows, bank, col) in enumerate(CHAN_BLOCKS):
                last = nc.tensor.transpose(ps[:, bank, col:col + rows], chan_stage[0:rows, k, :], ident[0:rows, 0:rows])
            last.then_inc(chanT, 1)
            transposes(gm_rows, 0)
            pe.wait_ge(wif_ready, 1)
            for k in range(KT):
                pe.wait_ge(h_done, k + 1)
                last = three(ps[:, 7, 0:T], hm_hi[:, k, 0:P], hm_lo[:, k, 0:P], h_hi[:, k, :], h_lo[:, k, :],
                             start=k == 0, stop=k == KT - 1)
            last.then_inc(gates_psum, 1)

            with pe.Fori(0, TURNS_MIX) as g:
                for u in range(U_MIX):
                    c = u // UNITS_CHUNK
                    if u % UNITS_CHUNK == 0:
                        if c in (5, 6):
                            pe.wait_ge(read_dve, g * 2 + (c - 4))
                        else:
                            pe.wait_ge(read_act, g * 6 + (c + 1 if c < 5 else 6))
                    ready(g * U_MIX + (BASE_MIX + u))
                    if c in (2, 5):
                        unit_tokens(u, c % 2)
                    else:
                        unit_channels(u, c % 2, h_hi, h_lo)
                    if u == 17:
                        pe.wait_ge(read_act, g * 6 + 4)
                        pe.wait_ge(m_gated, g + 1)
                        pe.wait_ge(gates_sb, 1)
                        for j in range(2):
                            for m in range(2):
                                q, k = qT[:, 2 * j + m, :], kT[:, 2 * j + m, :]
                                bank = 4 + 2 * j + m
                                nc.tensor.matmul(ps[:, bank, 0:P], q[:, 0:P], k[:, 0:P], start=True, stop=True)
                                last = nc.tensor.matmul(ps[:, bank, P:P + T], q[:, P:T], k[:, 0:T], start=True, stop=True)
                            last.then_inc(a_score, 1)
                    if u == 24:
                        pe.wait_ge(a_prob, g * 2 + 2)
                        for j in range(2):
                            for b in range(3):
                                last = nc.tensor.transpose(ps[:, 4 + j, b * P:(b + 1) * P], prob[:, 2 * j, b * P:(b + 1) * P], ident)
                        last.then_inc(a_probT, 1)
                    if u == 27:
                        pe.wait_ge(a_probT_sb, g + 1)
                        pe.wait_ge(read_act, g * 6 + 5)
                        for j in range(2):
                            last = head_values(attnT[:, j, :], j)
                        last.then_inc(a_num, 1)
                    if u == 34:
                        pe.wait_ge(a_on, g + 1)
                        heads_out().then_inc(a_onT, 1)
                    if u == 45:
                        pe.wait_ge(qk_ready, g * 2 + 2)
                        pe.wait_ge(a_done, g + 1)
                        for j in range(2):
                            for s in range(2):
                                for dt in range(2):
                                    last = nc.tensor.matmul(ps[:, 4 + j, (0, 256)[s]:(256, 384)[s]],
                                                            kT[:, 2 * j + dt, s * P:(s + 1) * P], qT[:, 2 * j + dt, s * P:T],
                                                            start=dt == 0, stop=dt == 1)
                        last.then_inc(m_score, 1)
                    if u == 50:
                        pe.wait_ge(m_at, g + 1)
                        pe.wait_ge(read_act, g * 6 + 6)
                        for j in range(2):
                            head_values(prob[:, 2 + j, :], j)
                            for b, parts in ((0, (0,)), (1, (1, 2))):
                                for i, part in enumerate(parts):
                                    last = nc.tensor.matmul(ps[:, 4 + j, 384 + b:385 + b], prob[:, 2 + j, part * P:(part + 1) * P],
                                                            ones[:], start=i == 0, stop=i == len(parts) - 1)
                        last.then_inc(m_num, 1)
                    if u == 57:
                        pe.wait_ge(m_on, g + 1)
                        heads_out().then_inc(m_onT, 1)

            with pe.Fori(0, TURNS_BR) as g:
                for u in range(U_BR):
                    c = u // UNITS_CHUNK
                    if u == 0:
                        pe.wait_ge(ga_read, g + 1)
                        pe.wait_ge(m_gated, TURNS_MIX + 1)
                    if u == 8:
                        pe.wait_ge(bm_read, g + 1)
                        pe.wait_ge(read_act, 6 * TURNS_MIX + 1)
                        pe.wait_ge(m_done, TURNS_MIX)
                    if u == 16:
                        pe.wait_ge(ba_read, g + 1)
                        pe.wait_ge(read_act, 6 * TURNS_MIX + 2)
                        pe.wait_ge(a_done, TURNS_MIX)
                    ready(g * U_BR + (BASE_BR + u))
                    unit_channels(u, (2, 0, 1)[c], *((h_hi, h_lo), (hm_hi, hm_lo), (ha_hi, ha_lo))[c])

            def rows_unit(u, b, first, last):
                kslot, half = rows_place(u, first or last)
                hi, lo = last_split(u) if last else (w_hi[:, u % RING, :], w_lo[:, u % RING, :])
                for part in (ks_hi, ks_lo):
                    for n in range(2):
                        a = part[:, kslot, b * P:(b + 1) * P]
                        o = ps[:, 4 * b + half * 2 + n, :]
                        ins = nc.tensor.matmul(o, a, hi[:, n * 512:n * 512 + 512],
                                               start=first and kslot == 0 and part is ks_hi,
                                               stop=last and kslot == 3 and part is ks_lo, skip_group_check=True)
                        if part is ks_hi:
                            nc.tensor.matmul(o, a, lo[:, n * 512:n * 512 + 512],
                                             start=False, stop=False, skip_group_check=True)
                return ins

            def rows_phase(turns, per_turn, base, tiles_before, bank_waits):
                def waits(g, u, first, last=False):
                    k, half = rows_place(u, first or last)
                    if first and k == 0:
                        bank_waits(half)
                    if half == 0:
                        pe.wait_ge(ks_done, g * 4 + (tiles_before + k + 1))
                    ready(g * per_turn + (base + u))

                def turn(g, first):
                    for u in range(per_turn):
                        waits(g, u, first)
                        for b in range(TB):
                            ins = rows_unit(u, b, first, False)
                        ins.then_inc(pe_done, 1)

                turn(0, True)
                with pe.Fori(1, turns - 1) as g:
                    turn(g, False)
                for b in range(TB):
                    for u in range(per_turn):
                        if b == 0:
                            waits(turns - 1, u, False, True)
                        ins = rows_unit(u, b, False, True)
                        if b == TB - 1:
                            ins.then_inc(pe_done, 1)
                        elif u % 4 == 3:
                            ins.then_inc(half_done, 1)

            def out_banks(half):
                if half == 0:
                    pe.wait_ge(ga_read, TURNS_BR + 1)
                    pe.wait_ge(bm_read, TURNS_BR + 1)
                    pe.wait_ge(m_on, TURNS_MIX)
                else:
                    pe.wait_ge(ba_read, TURNS_BR + 1)

            rows_phase(TURNS_OUT, U_OUT, BASE_OUT, 0, out_banks)
            transposes(xn, KT)
            with pe.Fori(0, TURNS_UP) as g:
                for u in range(U_UP):
                    if u == 0:
                        pe.wait_ge(gate_read, g * 2 + 1)
                    if u == 8:
                        pe.wait_ge(val_read, g + 1)
                    if u < UNITS_CHUNK:
                        pe.wait_ge(h_done, KT + 2 * u + 2)
                    ready(g * U_UP + (BASE_UP + u))
                    unit_channels(u, u // UNITS_CHUNK, h_hi, h_lo)

            def down_banks(half):
                pe.wait_ge(*((gate_read, 2 * TURNS_UP + 1) if half == 0 else (val_read, TURNS_UP + 1)))

            rows_phase(TURNS_DOWN, U_DOWN, BASE_DOWN, KT, down_banks)


_INS = ['x', 'w_in', 'w_branch_m', 'w_branch_a', 'w_out', 'g_post_mix', 'w_up', 'w_down', 'g_post_ffn']


def kernel(**inputs):
    import concourse.bacc as bacc
    from concourse.bass_utils import run_bass_kernel_spmd

    nc = bacc.Bacc("TRN2", target_bir_lowering=False, num_devices=1)
    arrays, args = {}, []
    inputs = {name: np.ascontiguousarray(a) for name, a in inputs.items()}
    laid = {name: inputs[name] for name in _INS}
    laid["channel_rows"] = channel_rows(inputs)
    laid["lambdas"] = np.concatenate([inputs[n][0] for n in ("lambda_q1", "lambda_q2", "lambda_k1", "lambda_k2")])
    laid["shape_constants"] = shape_constants()
    for name, a in laid.items():
        arrays[f"in_{name}"] = a
        args.append(nc.dram_tensor(f"in_{name}", a.shape, mybir.dt.from_np(a.dtype), kind="ExternalInput").ap())
    args.append(nc.dram_tensor("out", (1, T, D), F32, kind="ExternalOutput").ap())
    build_layer(nc, *args)
    r = run_bass_kernel_spmd(nc, [arrays], core_ids=[0])
    return r.results[0]["out"]
```
